# Optimizing a Trainium2 kernel written in Bass

```python
import jax, jax.numpy as jnp
from jax import lax
import numpy as np

D_MODEL = 1024
BATCH = 1
SEQ = 256
DEPTH = 2

N_A_LAYERS = DEPTH // 2
N_B_LAYERS = DEPTH - N_A_LAYERS
N_DENSE_LAYERS = (DEPTH + 1) // 2
N_MOE_LAYERS = DEPTH // 2

A_HEADS = 8
A_HEAD_DIM = D_MODEL // A_HEADS
A_WIDTH = A_HEADS * A_HEAD_DIM
A_CHUNK = 32

B_HEADS = 16
B_KV_HEADS = 4
B_GROUP = B_HEADS // B_KV_HEADS
B_HEAD_DIM = D_MODEL // B_HEADS
CMP_BLOCK = 32
CMP_STRIDE = 16
CMP_HIDDEN = 256
SEL_BLOCK = 32
N_SELECT = 8
WINDOW = 512
Q_BLOCK = 64
N_BRANCH = 3

D_FF = 2816
N_EXPERTS = 8
TOP_K = 2
D_FF_EXPERT = 3584

NORM_EPS = 1e-6
SEL_BIG = 1e9
TINY = 1e-30

kernel_name = "yoco_hgrn2_nsa_moe_trunk"

def rms_norm(x, g):
    xf = x.astype(jnp.float32)
    y = xf * lax.rsqrt(jnp.mean(xf * xf, axis=-1, keepdims=True) + NORM_EPS)
    return (y * g.astype(jnp.float32)).astype(x.dtype)

def masked_softmax(s, mask):
    s = jnp.where(mask, s, -jnp.inf)
    m = jnp.max(s, axis=-1, keepdims=True)
    m = jnp.where(jnp.isfinite(m), m, 0.0)
    e = jnp.exp(s - m)
    return e / jnp.maximum(jnp.sum(e, axis=-1, keepdims=True), TINY)

def alibi_slopes(n):
    return np.array([2.0 ** (-8.0 * (h + 1) / n) for h in range(n)], dtype=np.float32)

def hgrn2_lower_bounds(lb_logits):
    lb = jnp.cumsum(jax.nn.softmax(lb_logits.astype(jnp.float32), axis=0), axis=0)
    return lb - lb[0:1]

def hgrn2_chunk_scan(q, k, v, logf):
    B, H, S, dk = q.shape
    dv = v.shape[-1]
    nc = S // A_CHUNK

    def to_chunks(a):
        return a.reshape(B, H, nc, A_CHUNK, a.shape[-1]).transpose(2, 0, 1, 3, 4)

    causal = jnp.tril(jnp.ones((A_CHUNK, A_CHUNK), dtype=bool))[:, :, None]

    def step(state, inp):
        qc, kc, vc, lf = inp
        cum = jnp.cumsum(lf, axis=2)
        o_inter = jnp.einsum('bhtk,bhkv->bhtv', qc * jnp.exp(cum), state)
        diff = cum[:, :, :, None, :] - cum[:, :, None, :, :]
        decay = jnp.exp(jnp.where(causal, diff, -jnp.inf))
        scores = jnp.einsum('bhtk,bhsk,bhtsk->bhts', qc, kc, decay)
        o = o_inter + jnp.einsum('bhts,bhsv->bhtv', scores, vc)
        last = cum[:, :, -1:, :]
        new_state = (jnp.exp(last[:, :, 0, :])[..., None] * state
                     + jnp.einsum('bhsk,bhsv->bhkv', kc * jnp.exp(last - cum), vc))
        return new_state, o

    state0 = jnp.zeros((B, H, dk, dv), jnp.float32)
    _, o = lax.scan(step, state0, (to_chunks(q), to_chunks(k), to_chunks(v), to_chunks(logf)))
    return o.transpose(1, 2, 0, 3, 4).reshape(B, H, S, dv)

def hgrn2_mixer(xn, w_in, w_out, g_norm, lb):
    B, S, _ = xn.shape
    q, f, i, g = jnp.split(xn @ w_in, 4, axis=-1)
    f32 = f.astype(jnp.float32)
    logf = jnp.logaddexp(jnp.log(lb), jnp.log1p(-lb) + jax.nn.log_sigmoid(f32))
    key = (1.0 - lb) * jax.nn.sigmoid(-f32)

    def heads(a):
        return a.reshape(B, S, A_HEADS, A_HEAD_DIM).transpose(0, 2, 1, 3).astype(jnp.float32)

    o = hgrn2_chunk_scan(heads(jax.nn.silu(q)), heads(key), heads(i), heads(logf))
    o = rms_norm(o.transpose(0, 2, 1, 3), g_norm).reshape(B, S, A_WIDTH).astype(xn.dtype)
    return (o * jax.nn.silu(g)) @ w_out

def compress_blocks(a, pos, w1, w2):
    B, S = a.shape[:2]
    n_cmp = (S - CMP_BLOCK) // CMP_STRIDE + 1
    idx = np.arange(n_cmp)[:, None] * CMP_STRIDE + np.arange(CMP_BLOCK)[None, :]
    blocks = a[:, idx] + pos[None, None, :, None, :]
    blocks = blocks.transpose(0, 3, 1, 2, 4).reshape(B, B_KV_HEADS, n_cmp, CMP_BLOCK * B_HEAD_DIM)
    return jax.nn.silu(blocks @ w1) @ w2

def nsa_shared_kv(h, kv_norm, kv_w, cmp_pos_k, cmp_w1_k, cmp_w2_k, cmp_pos_v, cmp_w1_v, cmp_w2_v, k_norm):
    B, S, _ = h.shape
    hn = rms_norm(h, kv_norm)
    kv = (hn @ kv_w).reshape(B, S, 6, B_KV_HEADS, B_HEAD_DIM)
    k_c, v_c, k_s, v_s, k_w, v_w = (kv[:, :, 0], kv[:, :, 1], kv[:, :, 2], kv[:, :, 3], kv[:, :, 4], kv[:, :, 5])
    kc = rms_norm(compress_blocks(k_c, cmp_pos_k, cmp_w1_k, cmp_w2_k), k_norm[0])
    vc = compress_blocks(v_c, cmp_pos_v, cmp_w1_v, cmp_w2_v)
    n_sel = S // SEL_BLOCK
    ks = rms_norm(k_s, k_norm[1]).transpose(0, 2, 1, 3).reshape(B, B_KV_HEADS, n_sel, SEL_BLOCK * B_HEAD_DIM)
    vs = v_s.transpose(0, 2, 1, 3).reshape(B, B_KV_HEADS, n_sel, SEL_BLOCK * B_HEAD_DIM)
    pad = ((0, 0), (0, 0), (WINDOW, 0), (0, 0))
    kw = jnp.pad(rms_norm(k_w, k_norm[2]).transpose(0, 2, 1, 3), pad)
    vw = jnp.pad(v_w.transpose(0, 2, 1, 3), pad)
    return kc, vc, ks, vs, kw, vw

def nsa_mixer(xn, w_in, w_out, q_norm, kc, vc, ks, vs, kw, vw):
    B, S, _ = xn.shape
    dh = B_HEAD_DIM
    scale = dh ** -0.5
    n_cmp = kc.shape[2]
    n_sel = S // SEL_BLOCK
    n_pick = min(N_SELECT, n_sel)
    n_qb = S // Q_BLOCK
    c_start = np.arange(n_cmp) * CMP_STRIDE
    c_end = jnp.asarray(c_start + CMP_BLOCK - 1)
    j_sel = np.arange(n_sel)
    overlap = jnp.asarray(((c_start[:, None] < (j_sel[None, :] + 1) * SEL_BLOCK)
                           & (c_start[:, None] + CMP_BLOCK > j_sel[None, :] * SEL_BLOCK)).astype(np.float32))
    j_sel = jnp.asarray(j_sel)
    slopes = jnp.asarray(alibi_slopes(B_HEADS).reshape(B_KV_HEADS, B_GROUP))[None, None, :, :, None]
    gather = jax.vmap(jax.vmap(lambda a, i: a[i]))

    proj = xn @ w_in
    q = rms_norm(proj[..., :B_HEADS * dh].reshape(B, S, B_HEADS, dh), q_norm)
    gates = jax.nn.sigmoid(proj[..., B_HEADS * dh:].astype(jnp.float32)).astype(xn.dtype)
    q_blocks = jnp.moveaxis(q.reshape(B, n_qb, Q_BLOCK, B_KV_HEADS, B_GROUP, dh), 1, 0)
    g_blocks = jnp.moveaxis(gates.reshape(B, n_qb, Q_BLOCK, B_KV_HEADS, B_GROUP, N_BRANCH), 1, 0)

    def block(args):
        qb, gb, blk = args
        t = blk * Q_BLOCK + jnp.arange(Q_BLOCK)
        dist_c = t[:, None] - c_end[None, :]
        s_c = (jnp.einsum('bqghd,bgcd->bqghc', qb, kc, preferred_element_type=jnp.float32) * scale
               - slopes * dist_c.astype(jnp.float32)[None, :, None, None, :])
        p_c = masked_softmax(s_c, (dist_c >= 0)[None, :, None, None, :])
        o_c = jnp.einsum('bqghc,bgcd->bqghd', p_c.astype(vc.dtype), vc)
        imp = jnp.einsum('bqghc,cj->bqgj', p_c, overlap)
        valid = j_sel[None, :] * SEL_BLOCK <= t[:, None]
        cur = t // SEL_BLOCK
        forced = valid & ((j_sel[None, :] == 0) | (j_sel[None, :] == cur[:, None]) | (j_sel[None, :] == cur[:, None] - 1))
        score = jnp.where(forced[None, :, None, :], SEL_BIG, jnp.where(valid[None, :, None, :], imp, -SEL_BIG))
        vals, idx = lax.top_k(score, n_pick)
        sel_ok = vals > -0.5 * SEL_BIG
        idx_bg = idx.transpose(0, 2, 1, 3).reshape(B, B_KV_HEADS, Q_BLOCK * n_pick)
        k_sel = gather(ks, idx_bg).reshape(B, B_KV_HEADS, Q_BLOCK, n_pick * SEL_BLOCK, dh)
        v_sel = gather(vs, idx_bg).reshape(B, B_KV_HEADS, Q_BLOCK, n_pick * SEL_BLOCK, dh)
        pos_sel = idx[..., None] * SEL_BLOCK + jnp.arange(SEL_BLOCK)
        ok_sel = (sel_ok[..., None] & (pos_sel <= t[None, :, None, None, None])).reshape(B, Q_BLOCK, B_KV_HEADS, -1)
        dist_s = (t[None, :, None, None] - pos_sel.reshape(B, Q_BLOCK, B_KV_HEADS, -1)).astype(jnp.float32)
        s_s = (jnp.einsum('bqghd,bgqkd->bqghk', qb, k_sel, preferred_element_type=jnp.float32) * scale
               - slopes * dist_s[:, :, :, None, :])
        p_s = masked_softmax(s_s, ok_sel[:, :, :, None, :])
        o_s = jnp.einsum('bqghk,bgqkd->bqghd', p_s.astype(v_sel.dtype), v_sel)
        k_win = lax.dynamic_slice_in_dim(kw, blk * Q_BLOCK, WINDOW + Q_BLOCK, axis=2)
        v_win = lax.dynamic_slice_in_dim(vw, blk * Q_BLOCK, WINDOW + Q_BLOCK, axis=2)
        pos_w = blk * Q_BLOCK - WINDOW + jnp.arange(WINDOW + Q_BLOCK)
        dist_w = t[:, None] - pos_w[None, :]
        mask_w = (pos_w[None, :] >= 0) & (dist_w >= 0) & (dist_w < WINDOW)
        s_w = (jnp.einsum('bqghd,bgkd->bqghk', qb, k_win, preferred_element_type=jnp.float32) * scale
               - slopes * dist_w.astype(jnp.float32)[None, :, None, None, :])
        p_w = masked_softmax(s_w, mask_w[None, :, None, None, :])
        o_w = jnp.einsum('bqghk,bgkd->bqghd', p_w.astype(v_win.dtype), v_win)
        return gb[..., 0:1] * o_c + gb[..., 1:2] * o_s + gb[..., 2:3] * o_w

    o = lax.map(block, (q_blocks, g_blocks, jnp.arange(n_qb)))
    o = jnp.moveaxis(o, 0, 1).reshape(B, S, B_HEADS * dh)
    return o @ w_out

def swiglu(xn, w_gu, w_down):
    gate, up = jnp.split(xn @ w_gu, 2, axis=-1)
    return (jax.nn.silu(gate) * up) @ w_down

def moe_swiglu(xn, w_router, w_gu, w_down):
    logits = (xn @ w_router).astype(jnp.float32)
    vals, idx = lax.top_k(logits, TOP_K)
    wts = jax.nn.softmax(vals, axis=-1)
    combine = jnp.sum(jax.nn.one_hot(idx, N_EXPERTS, dtype=jnp.float32) * wts[..., None], axis=-2).astype(xn.dtype)
    out = jnp.zeros_like(xn)
    for e in range(N_EXPERTS):
        out = out + combine[..., e:e + 1] * swiglu(xn, w_gu[e], w_down[e])
    return out

def _normal(key, shape, scale):
    return jax.random.normal(key, shape, jnp.float32) * scale

def setup_inputs(seed: int = 0) -> dict:
    key = jax.random.key(seed)
    ks = jax.random.split(key, 25)
    dh = B_HEAD_DIM
    kv_cols = 6 * B_KV_HEADS * dh
    nsa_cols = B_HEADS * dh + N_BRANCH * B_HEADS
    return {
        "x": _normal(ks[0], (BATCH, SEQ, D_MODEL), 1.0),
        "norm_mix": 1.0 + _normal(ks[1], (DEPTH, D_MODEL), 0.02),
        "norm_ffn": 1.0 + _normal(ks[2], (DEPTH, D_MODEL), 0.02),
        "hgrn_w_in": _normal(ks[3], (N_A_LAYERS, D_MODEL, 4 * A_WIDTH), D_MODEL ** -0.5),
        "hgrn_w_out": _normal(ks[4], (N_A_LAYERS, A_WIDTH, D_MODEL), A_WIDTH ** -0.5),
        "hgrn_g_norm": 1.0 + _normal(ks[5], (N_A_LAYERS, A_HEAD_DIM), 0.02),
        "hgrn_lb_logits": _normal(ks[6], (N_A_LAYERS, A_WIDTH), 0.5),
        "kv_norm": 1.0 + _normal(ks[7], (D_MODEL,), 0.02),
        "kv_w": _normal(ks[8], (D_MODEL, kv_cols), D_MODEL ** -0.5),
        "cmp_pos_k": _normal(ks[9], (CMP_BLOCK, dh), 0.1),
        "cmp_w1_k": _normal(ks[10], (CMP_BLOCK * dh, CMP_HIDDEN), (CMP_BLOCK * dh) ** -0.5),
        "cmp_w2_k": _normal(ks[11], (CMP_HIDDEN, dh), CMP_HIDDEN ** -0.5),
        "cmp_pos_v": _normal(ks[12], (CMP_BLOCK, dh), 0.1),
        "cmp_w1_v": _normal(ks[13], (CMP_BLOCK * dh, CMP_HIDDEN), (CMP_BLOCK * dh) ** -0.5),
        "cmp_w2_v": _normal(ks[14], (CMP_HIDDEN, dh), CMP_HIDDEN ** -0.5),
        "k_norm": 1.0 + _normal(ks[15], (N_BRANCH, dh), 0.02),
        "nsa_w_in": _normal(ks[16], (N_B_LAYERS, D_MODEL, nsa_cols), D_MODEL ** -0.5),
        "nsa_w_out": _normal(ks[17], (N_B_LAYERS, B_HEADS * dh, D_MODEL), (B_HEADS * dh) ** -0.5),
        "nsa_q_norm": 1.0 + _normal(ks[18], (N_B_LAYERS, dh), 0.02),
        "ffn_w_gu": _normal(ks[19], (N_DENSE_LAYERS, D_MODEL, 2 * D_FF), D_MODEL ** -0.5),
        "ffn_w_down": _normal(ks[20], (N_DENSE_LAYERS, D_FF, D_MODEL), D_FF ** -0.5),
        "moe_router": _normal(ks[21], (N_MOE_LAYERS, D_MODEL, N_EXPERTS), D_MODEL ** -0.5),
        "moe_w_gu": _normal(ks[22], (N_MOE_LAYERS, N_EXPERTS, D_MODEL, 2 * D_FF_EXPERT), D_MODEL ** -0.5),
        "moe_w_down": _normal(ks[23], (N_MOE_LAYERS, N_EXPERTS, D_FF_EXPERT, D_MODEL), D_FF_EXPERT ** -0.5),
    }

def reference(x, norm_mix, norm_ffn, hgrn_w_in, hgrn_w_out, hgrn_g_norm, hgrn_lb_logits,
              kv_norm, kv_w, cmp_pos_k, cmp_w1_k, cmp_w2_k, cmp_pos_v, cmp_w1_v, cmp_w2_v, k_norm,
              nsa_w_in, nsa_w_out, nsa_q_norm, ffn_w_gu, ffn_w_down, moe_router, moe_w_gu, moe_w_down):
    lower_bounds = hgrn2_lower_bounds(hgrn_lb_logits)
    h = x
    kc = vc = ks = vs = kw = vw = None
    for layer in range(DEPTH):
        xn = rms_norm(h, norm_mix[layer])
        if layer < N_A_LAYERS:
            h = h + hgrn2_mixer(xn, hgrn_w_in[layer], hgrn_w_out[layer], hgrn_g_norm[layer], lower_bounds[layer])
        else:
            if layer == N_A_LAYERS:
                kc, vc, ks, vs, kw, vw = nsa_shared_kv(h, kv_norm, kv_w, cmp_pos_k, cmp_w1_k, cmp_w2_k,
                                                       cmp_pos_v, cmp_w1_v, cmp_w2_v, k_norm)
            j = layer - N_A_LAYERS
            h = h + nsa_mixer(xn, nsa_w_in[j], nsa_w_out[j], nsa_q_norm[j], kc, vc, ks, vs, kw, vw)
        xn = rms_norm(h, norm_ffn[layer])
        if layer % 2 == 0:
            h = h + swiglu(xn, ffn_w_gu[layer // 2], ffn_w_down[layer // 2])
        else:
            h = h + moe_swiglu(xn, moe_router[layer // 2], moe_w_gu[layer // 2], moe_w_down[layer // 2])
    return h


_drawn_inputs = setup_inputs


def setup_inputs(seed=0):
    import zlib

    import numpy as np

    out = dict(_drawn_inputs(seed))
    spreads = {}
    factors = {'hgrn_g_norm': 3.165,
     'kv_norm': 5.166,
     'cmp_pos_k': 5.886,
     'k_norm': 4.073,
     'nsa_q_norm': 8.0,
     'cmp_pos_v': 7.895}
    for name, (base, spread) in spreads.items():
        noise = np.random.default_rng([zlib.crc32(name.encode()), seed]).standard_normal(out[name].shape)
        drawn = base * np.exp(spread * noise) if base else spread * noise
        out[name] = __import__('jax').numpy.asarray(drawn.astype(out[name].dtype))
    for name, factor in factors.items():
        out[name] = (out[name] * factor).astype(out[name].dtype)
    return out
```

```python
from contextlib import ExitStack

import concourse.bass as bass
import numpy as np
from concourse import mybir

F32 = mybir.dt.float32
BF16 = mybir.dt.bfloat16
U8 = mybir.dt.uint8
I32 = mybir.dt.int32
ALU = mybir.AluOpType
ACT = mybir.ActivationFunctionType
AX = mybir.AxisListType

P = 128
T, D = 256, 1024
TB, KD = T // P, D // P
NH_A, DH_A = 8, 128
NH, NG, GRP, DH = 16, 4, 4, 64
DA = DH + 2
FF, FFE, NE = 2816, 3584, 8
CB, CS, NCMP, CH = 32, 16, 15, 256
EPS, TINY, NEG = 1e-6, 1e-30, -1e30

SLOTS = 7
ARENA = 16384
ITEM = 4096
N_HGRN_IN, N_HGRN_OUT, N_GU, N_DOWN, N_KV, N_CMP, N_Q, N_OUT = 8, 2, 11, 6, 3, 2, 2, 2
I_HOUT = N_HGRN_IN
I_GU = I_HOUT + N_HGRN_OUT
I_DOWN = I_GU + N_GU
I_KV = I_DOWN + N_DOWN
I_CMP = I_KV + N_KV
I_Q = I_CMP + N_CMP
I_OUT = I_Q + N_Q
I_MOE = I_OUT + N_OUT
NCH = FFE // 512
PER_E = 3 * NCH

C_ID, C_IOTA, C_TRI = 0, 128, 256
C_QPOS = 384
C_KPOS = C_QPOS + TB * NH * 2
C_CMASK = C_KPOS + TB * 2
C_CPOS = C_CMASK + TB * 32
C_TIE = C_CPOS + 2
C_HALF = C_TIE + 64
C_ONE = C_HALF + 8
C_ALL = C_ONE + 1

LEVELS = [0, 1, 2, 4, 8, 16, 32, 64, 128]
MLEV = 8

G_MIX0, G_MIX1, G_FFN0, G_FFN1, G_KV, G_HG = 0, 8, 16, 24, 32, 40
R_GAIN = 41
GQ, GK = 0, 1


def constants():
    f = np.zeros((P, C_ALL), np.float32)
    p = np.arange(P)
    f[:, C_ID:C_ID + P] = np.eye(P)
    f[:, C_IOTA:C_IOTA + P] = p
    f[:, C_TRI:C_TRI + P] = p[:, None] < p[None, :]
    f[:, C_ONE] = 1.0
    slope = np.array([2.0 ** (-8.0 * (h + 1) / NH) for h in range(NH)], np.float32)
    for tb in range(TB):
        t = (tb * P + p).astype(np.float32)
        for h in range(NH):
            f[:, C_QPOS + (tb * NH + h) * 2] = -slope[h] * t
            f[:, C_QPOS + (tb * NH + h) * 2 + 1] = slope[h]
        f[:, C_KPOS + tb * 2] = 1.0
        f[:, C_KPOS + tb * 2 + 1] = t
        for c in range(32):
            seen = (t >= c * CS + CB - 1) & (c < NCMP)
            f[:, C_CMASK + tb * 32 + c] = np.where(seen, 0.0, NEG)
    f[:, C_CPOS] = 1.0
    f[:, C_CPOS + 1] = (p % 32) * CS + CB - 1
    f[:, C_TIE:C_TIE + 64] = (np.arange(8)[None, :] < np.arange(8)[:, None]).reshape(1, 64)
    f[:, C_HALF:C_HALF + 8] = -0.5
    m = np.zeros((P, MLEV, P), np.float32)
    s, t = p[:, None], p[None, :]
    for n, lev in enumerate(LEVELS[:MLEV]):
        if lev == 0:
            m[:, n] = s == t
        else:
            m[:, n] = (s // (2 * lev) == t // (2 * lev)) & (s % (2 * lev) < lev) & (t % (2 * lev) >= lev)
    causal = np.where(s >= t, 0.0, NEG)
    return f, np.concatenate([m.reshape(P, MLEV * P), causal], 1).astype(np.float32)


class Steps:

    def __init__(self, eng, sem):
        self.eng, self.sem, self.n, self.loop = eng, sem, 0, None

    def __call__(self, ins):
        self.n += 1
        ins.then_inc(self.sem, 1)
        self.eng.wait_ge(self.sem, self.n if self.loop is None else self.loop + self.n)


def trunk(nc, x, norm_mix, norm_ffn, hgrn_w_in, hgrn_w_out, hgrn_g_norm, kv_norm, kv_w,
          cmp_pos_k, cmp_w1_k, cmp_w2_k, cmp_pos_v, cmp_w1_v, cmp_w2_v, k_norm,
          nsa_w_in, nsa_w_out, nsa_q_norm, ffn_w_gu, ffn_w_down, moe_router, moe_w_gu, moe_w_down,
          const_f32, const_masks, out):
    with ExitStack() as ctx:
        def sb(name, shape, dt=F32):
            return ctx.enter_context(nc.sbuf_tensor(name, shape, dt))

        def sem(name):
            return ctx.enter_context(nc.semaphore(name))

        ring = sb("ring", [P, SLOTS, ITEM])
        h = sb("h", [P, TB, D])
        xs = sb("xs", [P, TB, D])
        xT = sb("xT", [P, KD, T])
        cf = sb("cf", [P, C_ALL])
        cu = sb("cu", [P, MLEV, P], U8)
        cb = sb("cb", [P, 2 * P], BF16)
        gain = sb("gain", [P, 48])
        gnar = sb("gnar", [P, 4])
        small = sb("small", [P, 512])
        arena = sb("arena", [P, ARENA])
        bank = ctx.enter_context(nc.psum_tensor("bank", [P, 8, 512], F32))

        class Area:

            def __init__(self, at=0):
                self.at = at

            def __call__(self, *dims):
                n = int(np.prod(dims))
                v = arena[:, self.at:self.at + n]
                self.at += n
                assert self.at <= ARENA, self.at
                if len(dims) == 1:
                    return v
                names = "abcd"[:len(dims)]
                kw = {names[i]: dims[i] for i in range(1, len(dims))}
                return v.rearrange(f"p ({' '.join(names)}) -> p {' '.join(names)}", **kw)

        ident = cf[:, C_ID:C_ID + P]

        A = Area()
        a_q, a_k, a_c = A(NH_A, T), A(NH_A, T), A(NH_A, T)
        a_x, a_ql, a_kl = A(NH_A, T), A(NH_A, T), A(NH_A, T)
        a_st = A(2, TB, 4, P)
        a_v = A(TB, D)
        a_so = xT[:, 0:4, :].rearrange("p k t -> p (k t)").rearrange("p (g j t) -> p g j t", g=2, j=4)
        a_sg = xs
        a_oT = arena[:, 4 * 2048:5 * 2048].rearrange("p (k t) -> p k t", k=KD)
        a_on = arena[:, 3 * 2048:4 * 2048].rearrange("p (b n) -> p b n", b=TB)
        a_sq = arena[:, 5 * 2048:6 * 2048].rearrange("p (b n) -> p b n", b=4)
        A = Area()
        f_hT = A(2 * N_GU, T)
        f_sl = A(4, 256)
        f_hm = A(2, TB, 256)
        A = Area()
        b_xk = A(KD, T)
        b_qT = A(NH, T)
        b_kT = A(2, NG, T)
        b_v = A(2, TB, NG * DH)
        b_kc = A(P)
        b_vc = A(DH)
        b_o = A(TB, D)
        b_cin = b_o.rearrange("p b n -> p (b n)")[:, 0:CB * NG * NCMP].rearrange("p (j g c) -> p j g c", g=NG, c=NCMP)
        b_gate = A(TB, 48)
        U = A.at
        b_aug = A(2, 8, DA)
        b_sq = A(512)
        b_cT = A(NG, T)
        b_raw = xs
        b_w2 = A(2, 2, DH)
        b_pos = A(P)
        b_posT = A(CB)
        b_hid = A(2, 2, P)
        b_kca = A(DA)
        b_wg = A(KD, 48)
        A = Area(U)
        b_p = A(2, 4, T)
        b_pT = A(2, 8, P)
        b_t = arena[:, 0:256]
        b_cp = A(NH, 32)
        b_cpT = b_pT
        A = Area()
        m_sel, m_pos, m_wt = A(TB, NE), A(2 * TB, NE), A(TB, NE)
        m_cmp = A(NE, NE)
        m_cmp2 = A(NE, NE)
        m_lg = A(TB, NE)
        m_wr = A(KD, NE)
        m_P = A(TB, P)
        m_PW = A(TB, P)
        m_PT = A(T)
        m_x = A(KD, P)
        m_sl = A(2, 512)
        m_h = A(2, 512)
        m_hT = A(2, 4, P)
        m_y = A(D)
        flag = sb("flag", [P, 1], I32)

        slot_full = [sem(f"slot_full{s}") for s in range(SLOTS)]
        down_used = sem("down_used")
        x_in, const_in, gain_in, misc_in, wr_in = (sem(n) for n in ("x_in", "const_in", "gain_in", "misc_in", "wr_in"))
        gains_ps, gains_ok = sem("gains_ps"), sem("gains_ok")
        h_ready = sem("h_ready")
        ss_ready, rs_ready, xs_ready = sem("ss_ready"), sem("rs_ready"), sem("xs_ready")
        xT_ps, xT_dve, xT_act = sem("xT_ps"), sem("xT_dve"), sem("xT_act")
        proj_ready, f_absd, f_logged, f_lf, f_taken, key_ok, qv_taken = (
            sem(n) for n in ("proj_ready", "f_absd", "f_logged", "f_lf", "f_taken", "key_ok", "qv_taken"))
        dist_ready, fac_ready, ops_ready, pair_ps, pair_taken, zeroed = (
            sem(n) for n in ("dist_ready", "fac_ready", "ops_ready", "pair_ps", "pair_taken", "zeroed"))
        o_ps, osq_ready, oss_ready, ors_ready, on_ready, oT_ps, oT_dve, oT_act = (
            sem(n) for n in ("o_ps", "osq_ready", "oss_ready", "ors_ready", "on_ready", "oT_ps", "oT_dve", "oT_act"))
        sg_ready, res_ps = sem("sg_ready"), sem("res_ps")
        gu_ps, sl_ready, hm_ready, hT_ps, hT_ready = (
            sem(n) for n in ("gu_ps", "sl_ready", "hm_ready", "hT_ps", "hT_ready"))
        o_added, kv_ps, kv_sq, kv_ss, kv_rs, kv_norm_ok, kv_raw, kv_v = (
            sem(n) for n in ("o_added", "kv_ps", "kv_sq", "kv_ss", "kv_rs", "kv_norm_ok", "kv_raw", "kv_v"))
        kT_ps, kT_ready, cT_ps, cT_ready, cin_ready, hid_ps, hid_ready, kvc_ps, kvc_ready, kc_sq = (
            sem(n) for n in ("kT_ps", "kT_ready", "cT_ps", "cT_ready", "cin_ready", "hid_ps", "hid_ready", "kvc_ps", "kvc_ready", "kc_sq"))
        kc_ss, kc_rs, kca_ready, kcT_ps, kcT_ready, pos_ps, pos_ready = (
            sem(n) for n in ("kc_ss", "kc_rs", "kca_ready", "kcT_ps", "kcT_ready", "pos_ps", "pos_ready"))
        gate_ps, gate_exp, gate_ready = sem("gate_ps"), sem("gate_exp"), sem("gate_ready")
        q_ps, q_sq, q_ss, q_rs, qa_ready, qT_ps, qT_ready = (
            sem(n) for n in ("q_ps", "q_sq", "q_ss", "q_rs", "qa_ready", "qT_ps", "qT_ready"))
        cs_ps, cs_shift, cs_exp, cp_ready, cpT_ps, cpT_ready, co_ps, co_taken = (
            sem(n) for n in ("cs_ps", "cs_shift", "cs_exp", "cp_ready", "cpT_ps", "cpT_ready", "co_ps", "co_taken"))
        s_ps, max_ready, p_ready, pT_ps, pT_ready, av_ps, av_taken = (
            sem(n) for n in ("s_ps", "max_ready", "p_ready", "pT_ps", "pT_ready", "av_ps", "av_taken"))
        bo_ps, bo_dve, bo_act = sem("bo_ps"), sem("bo_dve"), sem("bo_act")
        lg_ps, lg_shift, lg_exp, sel_ready, rank_ps, route_ready = (
            sem(n) for n in ("lg_ps", "lg_shift", "lg_exp", "sel_ready", "rank_ps", "route_ready"))
        P_ready, x_ps, mx_dve, mx_act, PT_ps, PT_ready = (
            sem(n) for n in ("P_ready", "x_ps", "mx_dve", "mx_act", "PT_ps", "PT_ready"))
        e_gu, e_sl, e_h, e_hT_ps, e_hT, e_down, y_dve, y_act, sc_ps, sc_taken = (
            sem(n) for n in ("e_gu", "e_sl", "e_h", "e_hT_ps", "e_hT", "e_down", "y_dve", "y_act", "sc_ps", "sc_taken"))
        out_done = sem("out_done")
        dve_step, act_step, pool_step, dve_loop = sem("dve_step"), sem("act_step"), sem("pool_step"), sem("dve_loop")
        init_ok, masks_ok = sem("init_ok"), sem("masks_ok")
        S_SS, S_MS, S_RS = 0, 8, 16
        S_O = 32
        S_K = 96
        S_Q = 160
        S_C = 272
        S_CM = 288
        S_A = 400
        S_L = 440

        block = ctx.enter_context(nc.Block())

        def slot(i):
            return ring[:, i % SLOTS, :]

        def halves(v, m):
            return v.rearrange("p n t -> p (n t)").rearrange("p (b w m) -> p b w m", w=2, m=m)

        def full(i):
            return 32 * (i // SLOTS + 1)

        def left(i):
            if i < I_HOUT:
                return proj_ready, 2 * i + 2
            if i < I_GU:
                return res_ps, 2 * (i - I_HOUT) + 2
            if i < I_DOWN:
                return gu_ps, 2 * (i - I_GU) + 2
            if i < I_KV - 1:
                return down_used, i - I_DOWN + 1
            if i < I_KV:
                return res_ps, 8
            if i < I_CMP:
                return kv_ps, 2 * (i - I_KV) + 2
            if i < I_Q:
                return hid_ps, 2
            if i < I_OUT:
                return q_ps, 2 * (i - I_Q) + 2
            return res_ps, 8 + 2 * (i - I_OUT) + 2

        def gu_item(c, half):
            return half if c == 0 else 3 * c - 1 + half

        def down_item(c):
            return 3 * c + 4 if c < NCH - 1 else PER_E - 1

        expert_items = sorted([(gu_item(c, g), "gate up".split()[g], c) for c in range(NCH) for g in range(2)]
                              + [(down_item(c), "down", c) for c in range(NCH)])

        def expert_left(n, E):
            _, kind, c = expert_items[n]
            if kind == "down":
                return e_down, E * NCH + (c + 1)
            return e_gu, E * (2 * NCH) + (2 * c + 1 + (kind == "up"))

        @block.sync
        def _(sp):
            sp.dma_start(h[:, 0, :], x[0, 0:P, :]).then_inc(x_in, 16)
            sp.dma_start(h[:, 1, :], x[0, P:T, :]).then_inc(x_in, 16)
            i = 0

            def load(parts):
                nonlocal i
                if i >= SLOTS:
                    sp.wait_ge(*left(i - SLOTS))
                for dst, src in parts:
                    sp.dma_start(dst, src).then_inc(slot_full[i % SLOTS], 16)
                i += 1

            def columns(w, c0):
                dst = slot(i).rearrange("p (k c) -> p k c", k=KD)
                src = w[:, c0:c0 + 512].rearrange("(k p) c -> p k c", p=P)
                return [(dst[:, 4 * a:4 * a + 4, :], src[:, 4 * a:4 * a + 4, :]) for a in range(2)]

            w = hgrn_w_in[0]
            for part in (1, 0, 2, 3):
                for c in range(2):
                    load(columns(w, part * D + c * 512))
            for c in range(2):
                load(columns(hgrn_w_out[0], c * 512))
            for n in range(N_GU):
                dst = slot(i).rearrange("p (k g c) -> p k g c", k=KD, g=2)
                load([(dst[:, :, g, :], ffn_w_gu[0, :, g * FF + n * 256:g * FF + (n + 1) * 256]
                       .rearrange("(k p) c -> p k c", p=P)) for g in range(2)])
            for n in range(N_DOWN):
                b = min(4, FF // P - 4 * n)
                dst = slot(i).rearrange("p (b c) -> p b c", b=4)
                src = ffn_w_down[0, 4 * n * P:(4 * n + b) * P, :].rearrange("(b p) c -> p b c", p=P)
                load([(dst[:, 0:b, 512 * a:512 * a + 512], src[:, :, 512 * a:512 * a + 512]) for a in range(2)])
            for c in range(N_KV):
                load(columns(kv_w, c * 512))
            for a in range(N_CMP):
                dst = slot(i).rearrange("p (j c) -> p j c", j=16)
                load([(dst[DH * kv:DH * kv + DH, :, :],
                       w1[a * 16 * DH:(a + 1) * 16 * DH, :].rearrange("(j d) c -> d j c", d=DH))
                      for kv, w1 in enumerate((cmp_w1_k, cmp_w1_v))])
            for c in range(N_Q):
                load(columns(nsa_w_in[0], c * 512))
            for c in range(N_OUT):
                load(columns(nsa_w_out[0], c * 512))
            assert i == I_MOE

            def experts(e, E, first, last):
                for n in range(first, last):
                    _, kind, c = expert_items[n]
                    s = (I_MOE + n) % SLOTS
                    if n >= SLOTS:
                        sp.wait_ge(*expert_left(n - SLOTS, E))
                    elif isinstance(E, int) and E == 0:
                        sp.wait_ge(*left(I_MOE + n - SLOTS))
                    else:
                        sp.wait_ge(*expert_left(n - SLOTS + PER_E, E - 1))
                    for a in range(2):
                        if kind == "down":
                            dst = ring[:, s, :].rearrange("p (b c) -> p b c", b=4)[:, 2 * a:2 * a + 2, :]
                            src = moe_w_down[0, bass.ds(e, 1), c * 512 + a * 256:c * 512 + (a + 1) * 256, :]
                            src = src.rearrange("o (b p) c -> p (o b) c", p=P)
                        else:
                            c0 = (kind == "up") * FFE + c * 512
                            dst = ring[:, s, :].rearrange("p (k c) -> p k c", k=KD)[:, 4 * a:4 * a + 4, :]
                            src = moe_w_gu[0, bass.ds(e, 1), 512 * a:512 * a + 512, c0:c0 + 512]
                            src = src.rearrange("o (k p) c -> p (o k) c", p=P)
                        sp.dma_start(dst, src).then_inc(slot_full[s], 16)

            experts(0, 0, 0, SLOTS)
            with sp.Fori(0, NE - 1) as e:
                experts(e, e, SLOTS, PER_E)
                experts(e + 1, e + 1, 0, SLOTS)
            experts(NE - 1, NE - 1, SLOTS, PER_E)
            sp.wait_ge(route_ready, 3)
            most = sp.value_load(flag[0:1, 0:1], min_val=0, max_val=T)
            with sp.If(most > P):
                with sp.Fori(0, NE) as e:
                    experts(e, e + NE, 0, PER_E)

        @block.gpsimd
        def _(pool):
            step = Steps(pool, pool_step)
            pool.dma_start(cf[:], const_f32).then_inc(const_in, 16)
            masks = arena[:, 2048:2048 + (MLEV + 1) * P]
            pool.dma_start(masks, const_masks).then_inc(const_in, 16)
            pool.memset(a_st, 0.0).then_inc(zeroed, 1)
            pool.memset(a_ql, 0.0)
            pool.memset(a_kl, 0.0).then_inc(zeroed, 1)
            pool.wait_ge(const_in, 32)
            pool.tensor_copy(cu[:].rearrange("p m t -> p (m t)"), masks[:, 0:MLEV * P]).then_inc(masks_ok, 1)
            pool.tensor_copy(cb[:, 0:P], cf[:, C_ID:C_ID + P]).then_inc(masks_ok, 1)
            pool.tensor_copy(cb[:, P:2 * P], masks[:, MLEV * P:]).then_inc(masks_ok, 1)

            def inverse_rms(sums, n, width, got, count, told):
                pool.wait_ge(got, count)
                mean = small[:, sums + n:sums + 2 * n]
                step(pool.tensor_scalar(mean, small[:, sums:sums + n], 1.0 / width, EPS, ALU.mult, ALU.add))
                pool.tensor_tensor(small[:, sums + 2 * n:sums + 3 * n], mean,
                                   cf[:, C_HALF:C_HALF + n], ALU.pow).then_inc(told, 1)

            def norm(i):
                for tb in range(TB):
                    inverse_rms(S_SS + 3 * (2 * i + tb), 1, D, ss_ready, 2 * i + tb + 1, rs_ready)

            norm(0)
            for j in range(4):
                inverse_rms(S_O + 12 * j, 4, DH_A, oss_ready, j + 1, ors_ready)
            norm(1)
            norm(2)
            for j in range(4):
                inverse_rms(S_K + 12 * j, 4, DH, kv_ss, j + 1, kv_rs)
            inverse_rms(S_C, 1, DH, kc_ss, 1, kc_rs)
            for j in range(4):
                inverse_rms(S_Q + 24 * j, 8, DH, q_ss, j + 1, q_rs)
            norm(3)

        @block.scalar
        def _(act):
            step = Steps(act, act_step)
            g = arena[:, 0:128]
            for k, (w, r) in enumerate(((norm_mix, G_MIX0), (norm_ffn, G_FFN0))):
                act.dma_start(g[r:r + 16, :], w.rearrange("l (k p) -> (l k) p", p=P)).then_inc(gain_in, 16)
            act.dma_start(g[G_KV:G_KV + 8, :], kv_norm.rearrange("(k p) -> k p", p=P)).then_inc(gain_in, 16)
            act.dma_start(g[G_HG:G_HG + 1, :], hgrn_g_norm).then_inc(gain_in, 16)
            act.dma_start(arena[GQ:GQ + 1, 128:128 + DH], nsa_q_norm).then_inc(gain_in, 16)
            act.dma_start(arena[GK:GK + 3, 128:128 + DH], k_norm).then_inc(gain_in, 16)

            def norm(i, h_count):
                for tb in range(TB):
                    if i == 0:
                        act.wait_ge(x_in, 32)
                    else:
                        act.wait_ge(h_ready, h_count[tb])
                    act.activation(xs[:, tb, :], h[:, tb, :], ACT.Square,
                                   accum_out=small[:, S_SS + 3 * (2 * i + tb):S_SS + 3 * (2 * i + tb) + 1]
                                   ).then_inc(ss_ready, 1)

            def transposed(i, g0):
                for b in (1, 3):
                    act.wait_ge(xT_ps, 4 * i + b + 1)
                    for k in (2 * b, 2 * b + 1):
                        last = act.activation(xT[:, k, :], bank[:, b, 256 * (k % 2):256 * (k % 2) + 256],
                                              ACT.Copy, scale=gain[:, g0 + k:g0 + k + 1])
                last.then_inc(xT_act, 1)

            norm(0, None)
            act.wait_ge(gains_ok, 1)
            transposed(0, G_MIX0)
            for j in range(4):
                cc, xx = a_c[:, 2 * j:2 * j + 2, :], a_x[:, 2 * j:2 * j + 2, :]
                act.wait_ge(proj_ready, j + 1)
                step(act.activation(xx, bank[:, j, :], ACT.Abs))
                step(act.activation(xx, xx, ACT.Exp, scale=-1.0))
                act.activation(xx, xx, ACT.Ln, bias=1.0).then_inc(f_logged, 1)
            for j in range(4):
                kk = a_k[:, 2 * j:2 * j + 2, :]
                act.wait_ge(f_taken, j + 1)
                act.activation(kk, kk, ACT.Exp).then_inc(key_ok, 1)
            for j in range(4):
                act.wait_ge(proj_ready, 5 + j)
                act.activation(a_q[:, 2 * j:2 * j + 2, :], bank[:, j, :], ACT.Silu).then_inc(qv_taken, 1)
            act.wait_ge(xs_ready, 2)
            act.wait_ge(xT_ps, 4)
            u = 0
            for n in range(9):
                if n < 8:
                    act.wait_ge(proj_ready, 9 + n)
                    it, tb = divmod(n % 4, 2)
                    dst = (a_v if n < 4 else a_sg)[:, tb, 512 * it:512 * it + 512]
                    act.activation(dst, bank[:, n % 4, :], ACT.Copy).then_inc(qv_taken, 1)
                if n >= 1:
                    for grp in range(2):
                        m = LEVELS[n]
                        hs = slice(4 * grp, 4 * grp + 4)
                        cR = halves(a_c[:, hs, :], m)[:, :, 1, :]
                        xR = halves(a_x[:, hs, :], m)[:, :, 1, :]
                        xL = halves(a_x[:, hs, :], m)[:, :, 0, :]
                        u += 1
                        if m > 1:
                            act.wait_ge(dist_ready, u - 2)
                        last = act.activation(xR, cR, ACT.Exp)
                        if m > 1:
                            last = act.activation(xL, xL, ACT.Exp)
                        last.then_inc(fac_ready, 1)
            act.wait_ge(qv_taken, 12)
            act.activation(a_sg[:, :, :], a_sg[:, :, :], ACT.Silu).then_inc(sg_ready, 1)
            for j in range(4):
                act.wait_ge(o_ps, j + 1)
                act.wait_ge(pair_ps, 18)
                act.activation(a_sq[:, j, :], bank[:, j, :], ACT.Square).then_inc(osq_ready, 1)
            for b in (1, 3):
                act.wait_ge(oT_ps, b + 1)
                for k in (2 * b, 2 * b + 1):
                    last = act.activation(a_oT[:, k, :], bank[:, 4 + b, 256 * (k % 2):256 * (k % 2) + 256],
                                          ACT.Copy, scale=gain[:, G_HG:G_HG + 1])
            last.then_inc(oT_act, 1)
            norm(1, (3, 4))
            transposed(1, G_FFN0)
            for n in range(2 * N_GU):
                act.wait_ge(gu_ps, n + 1)
                if n >= 4:
                    act.wait_ge(hm_ready, n - 3)
                act.activation(f_sl[:, n % 4, :], bank[:, n % 4, 0:256], ACT.Silu).then_inc(sl_ready, 1)
            norm(2, (6, 8))
            act.dma_start(b_pos[0:CB, 0:DH], cmp_pos_k).then_inc(misc_in, 16)
            act.dma_start(b_pos[0:CB, DH:2 * DH], cmp_pos_v).then_inc(misc_in, 16)
            for kv, w2 in enumerate((cmp_w2_k, cmp_w2_v)):
                act.dma_start(b_w2[:, kv, :, :], w2.rearrange("(b p) d -> p b d", p=P)).then_inc(misc_in, 16)
            act.dma_start(b_wg, nsa_w_in[0, :, D:D + 48].rearrange("(k p) c -> p k c", p=P)).then_inc(misc_in, 16)
            transposed(2, G_MIX1)
            for j in range(6):
                it, tb = divmod(j, 2)
                act.wait_ge(kv_ps, j + 1)
                if it == 0:
                    act.activation(b_raw[:, tb, 0:512].rearrange("p (g v d) -> p v g d", v=2, g=NG),
                                   bank[:, j % 4, :].rearrange("p (v g d) -> p v g d", v=2, g=NG),
                                   ACT.Copy).then_inc(kv_raw, 1)
                else:
                    if j > 2:
                        act.wait_ge(kv_ss, j - 2)
                    step(act.activation(b_v[:, it - 1, tb, :], bank[:, j % 4, 256:512], ACT.Copy))
                    act.activation(b_sq[:, 0:256], bank[:, j % 4, 0:256], ACT.Square).then_inc(kv_sq, 1)
            act.wait_ge(init_ok, 1)
            for kv in range(2):
                act.wait_ge(hid_ps, kv + 1)
                for half in range(2):
                    last = act.activation(
                        b_hid[:, kv, half, :].rearrange("p (g c) -> p g c", g=NG)[:, :, 0:NCMP],
                        bank[:, 4 + kv, 64 * half:64 * half + 60].rearrange("p (g c) -> p g c", g=NG), ACT.Silu)
                last.then_inc(hid_ready, 1)
            act.wait_ge(kvc_ps, 2)
            act.wait_ge(kv_ss, 4)
            act.activation(b_sq[:, 0:DH], bank[:, 6, 0:DH], ACT.Square,
                           accum_out=small[:, S_C:S_C + 1]).then_inc(kc_ss, 1)
            act.wait_ge(gate_ps, 2)
            for tb in range(TB):
                act.activation(b_gate[:, tb, :], bank[:, 7, 64 * tb:64 * tb + 48], ACT.Exp, scale=-1.0).then_inc(gate_exp, 1)
            for j in range(4):
                act.wait_ge(q_ps, j + 1)
                act.wait_ge(kc_ss, 1)
                if j:
                    act.wait_ge(q_ss, j)
                act.activation(b_sq[:, :], bank[:, j, :], ACT.Square).then_inc(q_sq, 1)
            for tb in range(TB):
                act.wait_ge(cs_shift, tb + 1)
                act.activation(b_cp[:, :, :], b_cp[:, :, :], ACT.Exp).then_inc(cs_exp, 1)
            for u in range(16):
                tb, n = u % 2, P * (u % 2 + 1)
                act.wait_ge(max_ready, u + 1)
                if u >= 2:
                    act.wait_ge(pT_ps, u - 1)
                st = small[:, S_A + 16 * (u % 2):]
                for j in range(GRP):
                    src = (bank[:, 0, :].rearrange("p (j k) -> p j k", j=4) if tb == 0
                           else bank[:, 1:3, :].rearrange("p b (j k) -> p (b j) k", j=2))[:, j, 0:n]
                    last = act.activation(b_p[:, u % 2, j, 0:n], src, ACT.Exp,
                                          bias=small[:, S_A + 16 * (u % 2) + j:S_A + 16 * (u % 2) + j + 1],
                                          accum_out=small[:, S_A + 16 * (u % 2) + 4 + j:S_A + 16 * (u % 2) + 5 + j])
                last.then_inc(p_ready, 1)
            for b in (1, 3):
                act.wait_ge(bo_ps, b + 1)
                for k in (2 * b, 2 * b + 1):
                    last = act.activation(xT[:, k, :], bank[:, b, 256 * (k % 2):256 * (k % 2) + 256], ACT.Copy)
            last.then_inc(bo_act, 1)
            act.wait_ge(o_added, 16)
            act.dma_start(m_wr, moe_router[0].rearrange("(k p) c -> p k c", p=P)).then_inc(wr_in, 16)
            norm(3, (11, 12))
            transposed(3, G_FFN1)
            for tb in range(TB):
                act.wait_ge(lg_shift, tb + 1)
                act.activation(m_lg[:, tb, :], m_lg[:, tb, :], ACT.Exp).then_inc(lg_exp, 1)

            def experts(e, E):
                act.wait_ge(x_ps, E * 2 + 1)
                for k in range(4):
                    last = act.activation(m_x[:, k, :], bank[:, 7, P * k:P * k + P], ACT.Copy,
                                          scale=gain[:, G_FFN1 + k:G_FFN1 + k + 1])
                last.then_inc(mx_act, 1)
                act.wait_ge(PT_ps, E + 2)
                act.activation(m_PT[:, :], bank[:, 5, 0:T], ACT.Copy).then_inc(PT_ready, 1)
                for c in range(NCH + 1):
                    if c < NCH:
                        act.wait_ge(e_gu, E * (2 * NCH) + 2 * c + 1)
                        if c >= 2:
                            act.wait_ge(e_h, E * NCH + c - 1)
                        act.activation(m_sl[:, c % 2, :], bank[:, 2 * (c % 2), :], ACT.Silu).then_inc(e_sl, 1)
                    if c > 0:
                        act.wait_ge(e_hT_ps, E * NCH + (c + 1))
                        if c > 2:
                            act.wait_ge(e_down, E * NCH + (c - 2))
                        act.activation(m_hT[:, (c - 1) % 2, :, :], bank[:, 4, :], ACT.Copy).then_inc(e_hT, 1)
                act.wait_ge(e_down, E * NCH + NCH)
                act.activation(m_y[:, 512:1024], bank[:, 6, :], ACT.Copy).then_inc(y_act, 1)

            with act.Fori(0, NE) as e:
                experts(e, e)
            act.wait_ge(route_ready, 3)
            most = act.value_load(flag[0:1, 0:1], min_val=0, max_val=T)
            with act.If(most > P):
                with act.Fori(0, NE) as e:
                    experts(e, e + NE)
            act.wait_ge(h_ready, 13)
            for tb in range(TB):
                act.dma_start(out[0, tb * P:(tb + 1) * P, :], h[:, tb, :]).then_inc(out_done, 16)
            act.wait_ge(out_done, 32)

        @block.vector
        def _(dve):
            step = Steps(dve, dve_step)
            dve.wait_ge(const_in, 32)
            dve.wait_ge(gain_in, 96)
            dve.memset(arena[0:4, 128 + DH:128 + DA], 1.0).then_inc(gains_ps, 1)
            dve.wait_ge(gains_ps, 2)
            dve.tensor_copy(gain[:, 0:R_GAIN], bank[:, 4, 0:R_GAIN])
            dve.tensor_copy(gnar[0:DA, :], bank[0:DA, 4, 64:68]).then_inc(gains_ok, 1)
            dve.wait_ge(gains_ok, 1)
            step(dve.tensor_scalar(gnar[0:DH, GQ:GQ + 1], gnar[0:DH, GQ:GQ + 1], float(DH) ** -0.5, None, ALU.mult))

            def norm(i):
                for tb in range(TB):
                    dve.wait_ge(rs_ready, 2 * i + tb + 1)
                    dve.tensor_scalar(xs[:, tb, :], h[:, tb, :],
                                      small[:, S_SS + 3 * (2 * i + tb) + 2:S_SS + 3 * (2 * i + tb) + 3],
                                      None, ALU.mult).then_inc(xs_ready, 1)

            def transposed(i, g0, dst=xT, banks=(0, 2), told=xT_dve):
                for b in banks:
                    dve.wait_ge(xT_ps, 4 * i + b + 1)
                    for k in (2 * b, 2 * b + 1):
                        last = dve.tensor_scalar(dst[:, k, :], bank[:, b, 256 * (k % 2):256 * (k % 2) + 256],
                                                 gain[:, g0 + k:g0 + k + 1], None, ALU.mult)
                last.then_inc(told, 1)

            norm(0)
            transposed(0, G_MIX0)
            dve.wait_ge(masks_ok, 3)
            for j in range(4):
                cc, xx, kk = (v[:, 2 * j:2 * j + 2, :] for v in (a_c, a_x, a_k))
                dve.wait_ge(f_logged, j + 1)
                step(dve.scalar_tensor_tensor(cc, bank[:, j, :], 0.0, xx, ALU.min, ALU.subtract))
                dve.tensor_tensor(kk, cc, bank[:, j, :], ALU.subtract).then_inc(f_taken, 1)
            dve.wait_ge(zeroed, 2)
            dve.wait_ge(key_ok, 4)
            dve.wait_ge(qv_taken, 4)

            def take_pairs(n, grp):
                for tb in range(TB):
                    dve.wait_ge(pair_ps, 2 * n + grp + 1)
                    b = 4 + 2 * grp + tb
                    if n == MLEV:
                        if tb == 0:
                            dve.tensor_copy(a_so[:, grp, :, :], bank[:, b, :]).then_inc(pair_taken, 1)
                    else:
                        ins = dve.copy_predicated(a_st[:, grp, tb, :, :],
                                                  cu[:, n, :].unsqueeze(1).broadcast_to([P, 4, P]),
                                                  bank[:, b, :].rearrange("p (j t) -> p j t", j=4))
                        if tb:
                            ins.then_inc(pair_taken, 1)

            for n in range(1, 9):
                m = LEVELS[n]
                for grp in range(2):
                    hs = slice(4 * grp, 4 * grp + 4)
                    c_, x_, q_, k_, ql, kl = (halves(v[:, hs, :], m) for v in (a_c, a_x, a_q, a_k, a_ql, a_kl))
                    nb = 1024 // (2 * m)
                    end = c_[:, :, 0, m - 1:m].broadcast_to([P, nb, m])
                    if m > 1:
                        dve.tensor_tensor(x_[:, :, 0, :], end, c_[:, :, 0, :], ALU.subtract).then_inc(dist_ready, 1)
                for grp in range(2):
                    take_pairs(n - 1, grp)
                    hs = slice(4 * grp, 4 * grp + 4)
                    c_, x_, q_, k_, ql, kl = (halves(v[:, hs, :], m) for v in (a_c, a_x, a_q, a_k, a_ql, a_kl))
                    end = c_[:, :, 0, m - 1:m].broadcast_to([P, nb, m])
                    dve.wait_ge(fac_ready, 2 * (n - 1) + grp + 1)
                    last = dve.tensor_tensor(ql[:, :, 1, :], q_[:, :, 1, :], x_[:, :, 1, :], ALU.mult)
                    if m > 1:
                        last = dve.tensor_tensor(kl[:, :, 0, :], k_[:, :, 0, :], x_[:, :, 0, :], ALU.mult)
                    last.then_inc(ops_ready, 1)
                    if n < 8:
                        step(dve.tensor_tensor(c_[:, :, 1, :], c_[:, :, 1, :], end, ALU.add))
            for grp in range(2):
                take_pairs(8, grp)
            for j in range(4):
                tb, grp = divmod(j, 2)
                st = S_O + 12 * j
                dve.wait_ge(osq_ready, j + 1)
                dve.tensor_reduce(small[:, st:st + 4], a_sq[:, j, :].rearrange("p (n d) -> p n d", n=4),
                                  AX.X, ALU.add).then_inc(oss_ready, 1)
                dve.wait_ge(sg_ready, 1)
                dst = a_on[:, tb, 512 * grp:512 * grp + 512]
                step(dve.tensor_tensor(dst, bank[:, j, :], a_sg[:, tb, 512 * grp:512 * grp + 512], ALU.mult))
                dve.wait_ge(ors_ready, j + 1)
                d3 = dst.rearrange("p (n d) -> p n d", n=4)
                dve.tensor_tensor(d3, d3, small[:, st + 8:st + 12].unsqueeze(2).broadcast_to([P, 4, DH_A]),
                                  ALU.mult).then_inc(on_ready, 1)
            for b in (0, 2):
                dve.wait_ge(oT_ps, b + 1)
                for k in (2 * b, 2 * b + 1):
                    last = dve.tensor_scalar(a_oT[:, k, :], bank[:, 4 + b, 256 * (k % 2):256 * (k % 2) + 256],
                                             gain[:, G_HG:G_HG + 1], None, ALU.mult)
            last.then_inc(oT_dve, 1)

            def residual(first, order, b0=0):
                for j, (tb, half) in enumerate(order):
                    dve.wait_ge(res_ps, first + j + 1)
                    dst = h[:, tb, 512 * half:512 * half + 512]
                    dve.tensor_tensor(dst, dst, bank[:, b0 + j, :], ALU.add).then_inc(h_ready, 1)

            residual(0, [(tb, c) for c in range(2) for tb in range(TB)])
            norm(1)
            transposed(1, G_FFN0)
            for n in range(N_GU + 1):
                if n < N_GU:
                    for tb in range(TB):
                        j = 2 * n + tb
                        dve.wait_ge(sl_ready, j + 1)
                        if n >= 2:
                            dve.wait_ge(hT_ps, n - 1)
                        dve.tensor_tensor(f_hm[:, n % 2, tb, :], f_sl[:, j % 4, :], bank[:, j % 4, 256:512],
                                          ALU.mult).then_inc(hm_ready, 1)
                if n:
                    dve.wait_ge(hT_ps, n)
                    dve.tensor_copy(f_hT[:, 2 * n - 2:2 * n, :], bank[:, 4 + (n - 1) % 2, :]).then_inc(hT_ready, 1)
            residual(4, [(0, 0), (0, 1), (1, 0), (1, 1)])
            norm(2)
            transposed(2, G_MIX1)
            dve.wait_ge(xT_act, 3)
            transposed(2, G_KV, b_xk, (0, 1, 2, 3), xT_dve)

            def normed(j, n, width, job_sem, ss, rs, st, src, dst, told, pos):
                dve.wait_ge(job_sem, j + 1)
                dve.tensor_reduce(small[:, st:st + n], b_sq[:, 0:n * width].rearrange("p (n d) -> p n d", n=n),
                                  AX.X, ALU.add).then_inc(ss, 1)
                dve.wait_ge(rs, j + 1)
                dve.tensor_tensor(dst[:, :, 0:DH], src.rearrange("p (n d) -> p n d", n=n),
                                  small[:, st + 2 * n:st + 3 * n].unsqueeze(2).broadcast_to([P, n, DH]), ALU.mult)
                dve.tensor_copy(dst[:, :, DH:DA], pos).then_inc(told, 1)

            dve.memset(b_hid, 0.0).then_inc(init_ok, 1)
            for j in range(4):
                br, tb = divmod(j, 2)
                if j >= 2:
                    dve.wait_ge(kT_ps, j - 1)
                pos = cf[:, C_KPOS + 2 * tb:C_KPOS + 2 * tb + 2].unsqueeze(1).broadcast_to([P, NG, 2])
                normed(j, NG, DH, kv_sq, kv_ss, kv_rs, S_K + 12 * j, bank[:, (j + 2) % 4, 0:256],
                       b_aug[:, j % 2, 0:NG, :], kv_norm_ok, pos)
            for j in range(4):
                br, tb = divmod(j, 2)
                dve.wait_ge(kT_ps, j + 1)
                dve.tensor_scalar(b_kT[0:DA, br, :, P * tb:P * tb + P],
                                  bank[0:DA, 4 + j, :].rearrange("p (g t) -> p g t", g=NG),
                                  gnar[0:DA, GK + 1 + br:GK + 2 + br], None, ALU.mult).then_inc(kT_ready, 1)
            for tb in range(TB):
                dve.wait_ge(cT_ps, tb + 1)
                dve.tensor_copy(b_cT[:, :, P * tb:P * tb + P],
                                bank[:, tb, :].rearrange("p (g t) -> p g t", g=NG)).then_inc(cT_ready, 1)
            dve.wait_ge(pos_ps, 1)
            dve.tensor_copy(b_posT, bank[:, 2, 0:CB]).then_inc(pos_ready, 1)
            dve.wait_ge(cT_ready, 2)
            dve.wait_ge(pos_ready, 1)
            for g in range(NG):
                for par in range(2):
                    k = (NCMP + 1 - par) // 2
                    src = b_cT[:, g, CS * par:CS * par + 32 * k].rearrange("p (i j) -> p j i", j=32)
                    dst = b_cin[:, :, g, par:NCMP:2]
                    last = dve.tensor_tensor(dst, src, b_posT.unsqueeze(2).broadcast_to([P, CB, k]), ALU.add)
            last.then_inc(cin_ready, 1)
            dve.wait_ge(kc_rs, 1)
            dve.wait_ge(kvc_ps, 2)
            dve.tensor_copy(b_vc, bank[:, 6, DH:2 * DH]).then_inc(kvc_ready, 1)
            dve.tensor_scalar(b_kca[:, 0:DH], bank[:, 6, 0:DH], small[:, S_C + 2:S_C + 3], None, ALU.mult)
            dve.tensor_copy(b_kca[:, DH:DA], cf[:, C_CPOS:C_CPOS + 2]).then_inc(kca_ready, 1)
            dve.wait_ge(kcT_ps, 1)
            dve.tensor_scalar(b_kc[0:DA, :], bank[0:DA, 5, 0:P], gnar[0:DA, GK:GK + 1], None,
                              ALU.mult).then_inc(kcT_ready, 1)
            for tb in range(TB):
                dve.wait_ge(gate_exp, tb + 1)
                step(dve.tensor_scalar(b_gate[:, tb, :], b_gate[:, tb, :], 1.0, None, ALU.add))
                step(dve.reciprocal(b_gate[:, tb, :], b_gate[:, tb, :]))
            for j in range(5):
                if j < 4:
                    it, tb = divmod(j, 2)
                    if j >= 2:
                        dve.wait_ge(qT_ps, 2 * (j - 1))
                    else:
                        dve.wait_ge(kT_ps, 4)
                    pos = cf[:, C_QPOS + 2 * (NH * tb + 8 * it):C_QPOS + 2 * (NH * tb + 8 * it) + 16]
                    normed(j, 8, DH, q_sq, q_ss, q_rs, S_Q + 24 * j, bank[:, j, :], b_aug[:, j % 2, :, :],
                           qa_ready, pos.rearrange("p (n w) -> p n w", w=2))
                if j:
                    it, tb = divmod(j - 1, 2)
                    for a in range(2):
                        dve.wait_ge(qT_ps, 2 * (j - 1) + a + 1)
                        hh = 8 * it + 4 * a
                        dve.tensor_scalar(b_qT[0:DA, hh:hh + 4, P * tb:P * tb + P],
                                          bank[0:DA, 4 + (2 * (j - 1) + a) % 4, :].rearrange("p (n t) -> p n t", n=4),
                                          gnar[0:DA, GQ:GQ + 1], None, ALU.mult).then_inc(qT_ready, 1)
            for tb in range(TB):
                st = S_CM + 48 * tb
                cp = b_cp
                dve.wait_ge(cs_ps, tb + 1)
                if tb:
                    dve.wait_ge(cpT_ps, tb)
                step(dve.tensor_tensor(cp, bank[:, tb, :].rearrange("p (n c) -> p n c", n=NH),
                                       cf[:, C_CMASK + 32 * tb:C_CMASK + 32 * tb + 32].unsqueeze(1)
                                       .broadcast_to([P, NH, 32]), ALU.add))
                step(dve.tensor_reduce(small[:, st:st + 16], cp, AX.X, ALU.max))
                step(dve.tensor_scalar(small[:, st:st + 16], small[:, st:st + 16], NEG / 10, None, ALU.max))
                dve.tensor_tensor(cp, cp, small[:, st:st + 16].unsqueeze(2).broadcast_to([P, NH, 32]),
                                  ALU.subtract).then_inc(cs_shift, 1)
                dve.wait_ge(cs_exp, tb + 1)
                step(dve.tensor_reduce(small[:, st + 16:st + 32], cp, AX.X, ALU.add))
                step(dve.tensor_scalar(small[:, st + 16:st + 32], small[:, st + 16:st + 32], TINY, None, ALU.max))
                step(dve.reciprocal(small[:, st + 16:st + 32], small[:, st + 16:st + 32]))
                gt = b_gate[:, tb, :].rearrange("p (g j b) -> p j g b", g=NG, b=3)[:, :, :, 0]
                sj = small[:, st + 16:st + 32].rearrange("p (j g) -> p j g", j=GRP)
                step(dve.tensor_tensor(sj, sj, gt, ALU.mult))
                dve.tensor_tensor(cp, cp, small[:, st + 16:st + 32].unsqueeze(2).broadcast_to([P, NH, 32]),
                                  ALU.mult).then_inc(cp_ready, 1)
                dve.wait_ge(cpT_ps, tb + 1)
                dve.tensor_copy(b_cpT[:, tb, 0:4, :], bank[:, 2 + tb, :].rearrange("p (j t) -> p j t", j=4)
                                ).then_inc(cpT_ready, 1)
            for g in range(NG):
                dve.wait_ge(co_ps, 8)
                dve.tensor_copy(b_o[:, :, 256 * g:256 * g + 256],
                                bank[:, 4 + g, :].rearrange("p (b d) -> p b d", b=TB)).then_inc(co_taken, 1)
            dve.wait_ge(co_taken, 4)

            def add_out(u):
                br, g, tb = u // 8, u // 2 % 4, u % 2
                st = S_A + 16 * (u % 2)
                dve.wait_ge(av_ps, u + 1)
                o3 = b_o[:, tb, 256 * g:256 * g + 256].rearrange("p (j d) -> p j d", j=GRP)
                t3 = b_t.rearrange("p (j d) -> p j d", j=GRP)
                dve.tensor_tensor(t3, bank[:, 6 + u % 2, 0:256].rearrange("p (j d) -> p j d", j=GRP),
                                  small[:, st + 8:st + 12].unsqueeze(2).broadcast_to([P, GRP, DH]),
                                  ALU.mult).then_inc(av_taken, 1)
                dve.wait_ge(av_taken, u + 1)
                dve.tensor_tensor(o3, o3, t3, ALU.add).then_inc(o_added, 1)
                dve.wait_ge(o_added, u + 1)

            def probs(u):
                br, g, tb = u // 8, u // 2 % 4, u % 2
                st = S_A + 16 * (u % 2)
                dve.wait_ge(p_ready, u + 1)
                step(dve.reciprocal(small[:, st + 8:st + 12], small[:, st + 4:st + 8]))
                gt = b_gate[:, tb, :].rearrange("p (h b) -> p h b", b=3)[:, GRP * g:GRP * g + GRP, 1 + br]
                step(dve.tensor_tensor(small[:, st + 8:st + 12], small[:, st + 8:st + 12], gt, ALU.mult))
                dve.wait_ge(pT_ps, u + 1)
                if u >= 2:
                    dve.wait_ge(av_ps, u - 1)
                if tb == 0:
                    src, dst = bank[:, 3, :], b_pT[:, 0, 0:4, :]
                    src = src.rearrange("p (j t) -> p j t", j=4)
                else:
                    src, dst = bank[:, 4:6, :].rearrange("p b (j t) -> p (b j) t", j=4), b_pT[:, 1, :, :]
                dve.tensor_copy(dst, src).then_inc(pT_ready, 1)

            for u in range(17):
                if u < 16:
                    tb, n = u % 2, P * (u % 2 + 1)
                    st = S_A + 16 * (u % 2)
                    src = (bank[:, 0, :].rearrange("p (j k) -> p j k", j=4) if tb == 0
                           else bank[:, 1:3, :].rearrange("p b (j k) -> p (b j) k", j=2))
                    dve.wait_ge(s_ps, u + 1)
                    step(dve.tensor_reduce(small[:, st:st + 4], src, AX.X, ALU.max))
                    dve.tensor_scalar(small[:, st:st + 4], small[:, st:st + 4], -1.0, None, ALU.mult).then_inc(max_ready, 1)
                if u:
                    probs(u - 1)
                    add_out(u - 1)
            for b in (0, 2):
                dve.wait_ge(bo_ps, b + 1)
                for k in (2 * b, 2 * b + 1):
                    last = dve.tensor_copy(xT[:, k, :], bank[:, b, 256 * (k % 2):256 * (k % 2) + 256])
            last.then_inc(bo_dve, 1)
            residual(8, [(tb, c) for c in range(2) for tb in range(TB)], 4)
            norm(3)
            transposed(3, G_FFN1)
            for tb in range(TB):
                lg, sel, wt = m_lg[:, tb, :], m_sel[:, tb, :], m_wt[:, tb, :]
                dve.wait_ge(lg_ps, 2)
                step(dve.tensor_copy(lg, bank[:, 4, 8 * tb:8 * tb + 8]))
                mine, other = lg.unsqueeze(2).broadcast_to([P, NE, NE]), lg.unsqueeze(1).broadcast_to([P, NE, NE])
                step(dve.tensor_tensor(m_cmp, other, mine, ALU.is_equal))
                step(dve.tensor_tensor(m_cmp, m_cmp, cf[:, C_TIE:C_TIE + 64].rearrange("p (e j) -> p e j", e=NE), ALU.mult))
                step(dve.tensor_tensor(m_cmp2, other, mine, ALU.is_gt))
                step(dve.tensor_tensor(m_cmp, m_cmp, m_cmp2, ALU.add))
                step(dve.tensor_reduce(sel, m_cmp, AX.X, ALU.add))
                step(dve.tensor_scalar(sel, sel, 2.0, None, ALU.is_lt))
                step(dve.tensor_reduce(small[:, S_L + tb:S_L + tb + 1], lg, AX.X, ALU.max))
                dve.tensor_scalar(lg, lg, small[:, S_L + tb:S_L + tb + 1], None, ALU.subtract).then_inc(lg_shift, 1)
                dve.wait_ge(lg_exp, tb + 1)
                step(dve.tensor_tensor(wt, lg, sel, ALU.mult))
                step(dve.tensor_reduce(small[:, S_L + 2 + tb:S_L + 3 + tb], wt, AX.X, ALU.add))
                step(dve.reciprocal(small[:, S_L + 2 + tb:S_L + 3 + tb], small[:, S_L + 2 + tb:S_L + 3 + tb]))
                dve.tensor_scalar(wt, wt, small[:, S_L + 2 + tb:S_L + 3 + tb], None, ALU.mult).then_inc(sel_ready, 1)
            dve.wait_ge(rank_ps, 1)
            for q in range(2):
                ins = dve.tensor_scalar(m_pos[:, 2 * q:2 * q + 2, :], bank[:, 5, 0:16].rearrange("p (b e) -> p b e", b=TB),
                                        -float(P * q), None, ALU.add)
            ins.then_inc(route_ready, 1)
            dve.tensor_reduce(small[:, S_L + 4:S_L + 5], bank[:, 5, 16:24], AX.X, ALU.max).then_inc(route_ready, 1)
            dve.wait_ge(route_ready, 2)
            dve.tensor_copy(flag[:, :], small[:, S_L + 4:S_L + 5]).then_inc(route_ready, 1)

            for n, told in enumerate((PT_ps, e_hT_ps, e_hT, sc_taken)):
                dve.memset(small[:, 504 + n:505 + n], 0.0).then_inc(told, 1)

            def experts(e, E, q):
                iota = cf[:, C_IOTA:C_IOTA + P]
                dve.wait_ge(PT_ps, E + 1)
                for tb in range(TB):
                    dve.tensor_scalar(m_P[:, tb, :], iota, m_pos[:, 2 * q + tb, bass.ds(e, 1)],
                                      m_sel[:, tb, bass.ds(e, 1)], ALU.is_equal, ALU.mult).then_inc(dve_loop, 1)
                dve.wait_ge(dve_loop, E * 2 + 2)
                for tb in range(TB):
                    last = dve.tensor_scalar(m_PW[:, tb, :], m_P[:, tb, :], m_wt[:, tb, bass.ds(e, 1)],
                                             None, ALU.mult)
                last.then_inc(P_ready, 1)
                dve.wait_ge(x_ps, E * 2 + 2)
                for k in range(4, KD):
                    last = dve.tensor_scalar(m_x[:, k, :], bank[:, 4, P * (k - 4):P * (k - 3)],
                                             gain[:, G_FFN1 + k:G_FFN1 + k + 1], None, ALU.mult)
                last.then_inc(mx_dve, 1)
                for c in range(NCH):
                    dve.wait_ge(e_sl, E * NCH + c + 1)
                    dve.wait_ge(e_gu, E * (2 * NCH) + 2 * c + 2)
                    dve.wait_ge(e_hT_ps, E * NCH + (max(c - 1, 0) + 1))
                    dve.tensor_tensor(m_h[:, c % 2, :], m_sl[:, c % 2, :], bank[:, 2 * (c % 2) + 1, :],
                                      ALU.mult).then_inc(e_h, 1)
                dve.wait_ge(e_down, E * NCH + NCH)
                dve.tensor_copy(m_y[:, 0:512], bank[:, 5, :]).then_inc(y_dve, 1)
                for j in range(4):
                    tb, half = divmod(j, 2)
                    dve.wait_ge(sc_ps, E * 4 + j + 1)
                    dst = h[:, tb, 512 * half:512 * half + 512]
                    dve.tensor_tensor(dst, dst, bank[:, j, :], ALU.add).then_inc(sc_taken, 1)

            with dve.Fori(0, NE) as e:
                experts(e, e, 0)
            dve.wait_ge(route_ready, 3)
            most = dve.value_load(flag[0:1, 0:1], min_val=0, max_val=T)
            with dve.If(most > P):
                with dve.Fori(0, NE) as e:
                    experts(e, e + NE, 1)
            dve.memset(small[:, 500:501], 0.0).then_inc(h_ready, 1)

        @block.tensor
        def _(pe):
            mm, tp = nc.tensor.matmul, nc.tensor.transpose
            pe.wait_ge(const_in, 32)
            pe.wait_ge(gain_in, 96)
            pe.wait_ge(gains_ps, 1)
            tp(bank[:, 4, 0:R_GAIN], arena[0:R_GAIN, 0:P], ident[0:R_GAIN, 0:R_GAIN])
            tp(bank[0:DA, 4, 64:68], arena[0:4, 128:128 + DA], ident[0:4, 0:4]).then_inc(gains_ps, 1)

            def transposed(src, told, b0=0):
                for tb in range(TB):
                    for k in range(KD):
                        last = tp(bank[:, b0 + k // 2, 256 * (k % 2) + P * tb:256 * (k % 2) + P * tb + P],
                                  src[:, tb, P * k:P * k + P], ident)
                        if tb and k % 2:
                            last.then_inc(told, 1)

            def norm(i):
                for tb in range(TB):
                    pe.wait_ge(xs_ready, 2 * i + tb + 1)
                    for k in range(KD):
                        last = tp(bank[:, k // 2, 256 * (k % 2) + P * tb:256 * (k % 2) + P * tb + P],
                                  xs[:, tb, P * k:P * k + P], ident)
                        if tb and k % 2:
                            last.then_inc(xT_ps, 1)

            def arrived(i):
                pe.wait_ge(slot_full[i % SLOTS], full(i))

            def cols(i):
                return slot(i).rearrange("p (k c) -> p k c", k=KD)

            norm(0)
            pe.wait_ge(xT_dve, 1)
            pe.wait_ge(xT_act, 1)
            for j in range(8):
                i = j // 2
                if j % 2 == 0:
                    arrived(i)
                if j >= 4:
                    pe.wait_ge(f_taken, j - 3)
                for hh in range(2):
                    c0 = (2 * (j % 2) + hh) * P
                    for k in range(KD):
                        last = mm(bank[:, j % 4, 256 * hh:256 * hh + 256], cols(i)[:, k, c0:c0 + P],
                                  xT[:, k, :], start=k == 0, stop=k == KD - 1)
                last.then_inc(proj_ready, 1)

            def pairs(n, grp):
                m = LEVELS[n]
                if n == 0:
                    pe.wait_ge(key_ok, 4)
                    pe.wait_ge(qv_taken, 4)
                else:
                    pe.wait_ge(ops_ready, 2 * (n - 1) + grp + 1)
                    pe.wait_ge(pair_taken, 2 * (n - 1) + grp + 1)
                for tb in range(TB):
                    for hh in range(4):
                        hd = 4 * grp + hh
                        b = 4 + 2 * grp + tb
                        if n == MLEV:
                            if tb == 0:
                                last = mm(bank[:, b, P * hh:P * hh + P], a_kl[:, hd, 0:P], a_ql[:, hd, P:T],
                                          start=True, stop=True)
                            continue
                        ts = slice(P * tb, P * tb + P)
                        last = mm(bank[:, b, P * hh:P * hh + P], (a_kl if m > 1 else a_k)[:, hd, ts],
                                  (a_ql if m else a_q)[:, hd, ts], start=True, stop=True)
                last.then_inc(pair_ps, 1)

            for n in range(9):
                if n < 8:
                    it, tb = divmod(n, 2)
                    if tb == 0:
                        arrived(4 + it)
                    pe.wait_ge(qv_taken, n + 1)
                    for k in range(KD):
                        last = mm(bank[:, n % 4, :], xT[:, k, P * tb:P * tb + P], cols(4 + it)[:, k, :],
                                  start=k == 0, stop=k == KD - 1)
                    last.then_inc(proj_ready, 1)
                for grp in range(2):
                    pairs(n, grp)
            pe.wait_ge(qv_taken, 12)
            for j in range(4):
                tb, grp = divmod(j, 2)
                pe.wait_ge(pair_taken, 17 + grp)
                for hh in range(4):
                    cs = slice(512 * grp + P * hh, 512 * grp + P * hh + P)
                    dst = bank[:, j, P * hh:P * hh + P]
                    if tb:
                        mm(dst, a_so[:, grp, hh, :], a_v[:, 0, cs], start=True, stop=False)
                    last = mm(dst, a_st[:, grp, tb, hh, :], a_v[:, tb, cs], start=not tb, stop=True)
                last.then_inc(o_ps, 1)
            pe.wait_ge(on_ready, 4)
            transposed(a_on, oT_ps, 4)
            pe.wait_ge(oT_dve, 1)
            pe.wait_ge(oT_act, 1)

            def out_product(i0, lhs, b0=0):
                for c in range(2):
                    arrived(i0 + c)
                    for tb in range(TB):
                        for k in range(KD):
                            last = mm(bank[:, b0 + 2 * c + tb, :], lhs[:, k, P * tb:P * tb + P], cols(i0 + c)[:, k, :],
                                      start=k == 0, stop=k == KD - 1)
                        last.then_inc(res_ps, 1)

            out_product(I_HOUT, a_oT)
            pe.wait_ge(h_ready, 4)
            norm(1)
            pe.wait_ge(xT_dve, 2)
            pe.wait_ge(xT_act, 2)
            for n in range(N_GU + 1):
                if n < N_GU:
                    arrived(I_GU + n)
                    w = cols(I_GU + n)
                    for tb in range(TB):
                        j = 2 * n + tb
                        if j >= 4:
                            pe.wait_ge(hm_ready, j - 3)
                        for k in range(KD):
                            last = mm(bank[:, j % 4, :], xT[:, k, P * tb:P * tb + P], w[:, k, :],
                                      start=k == 0, stop=k == KD - 1)
                        last.then_inc(gu_ps, 1)
                if n:
                    pe.wait_ge(hm_ready, 2 * n)
                    if n > 2:
                        pe.wait_ge(hT_ready, n - 2)
                    for b in range(2):
                        for tb in range(TB):
                            last = tp(bank[:, 4 + (n - 1) % 2, 256 * b + P * tb:256 * b + P * tb + P],
                                      f_hm[:, (n - 1) % 2, tb, P * b:P * b + P], ident)
                    last.then_inc(hT_ps, 1)
            pe.wait_ge(hT_ready, N_GU)
            for n in range(N_DOWN):
                arrived(I_DOWN + n)
                w = slot(I_DOWN + n).rearrange("p (b c) -> p b c", b=4)
                nb = min(4, 2 * N_GU - 4 * n)
                for b in range(nb):
                    f = 4 * n + b
                    for tb in range(TB):
                        for c in range(2):
                            last = mm(bank[:, 2 * tb + c, :], f_hT[:, f, P * tb:P * tb + P], w[:, b, 512 * c:512 * c + 512],
                                      start=f == 0, stop=f == 2 * N_GU - 1)
                            if f == 2 * N_GU - 1:
                                last.then_inc(res_ps, 1)
                if n < N_DOWN - 1:
                    last.then_inc(down_used, 1)
            pe.wait_ge(h_ready, 8)
            norm(2)
            pe.wait_ge(xT_dve, 4)
            pe.wait_ge(xT_act, 3)
            for j in range(6):
                it, tb = divmod(j, 2)
                if tb == 0:
                    arrived(I_KV + it)
                if j >= 4:
                    pe.wait_ge(kv_raw, j - 3)
                for k in range(KD):
                    last = mm(bank[:, j % 4, :], b_xk[:, k, P * tb:P * tb + P], cols(I_KV + it)[:, k, :],
                              start=k == 0, stop=k == KD - 1)
                last.then_inc(kv_ps, 1)
            for j in range(4):
                pe.wait_ge(kv_norm_ok, j + 1)
                for g in range(NG):
                    last = tp(bank[0:DA, 4 + j, P * g:P * g + P], b_aug[:, j % 2, g, :], ident)
                last.then_inc(kT_ps, 1)
            pe.wait_ge(misc_in, 80)
            pe.wait_ge(kv_raw, 2)
            for tb in range(TB):
                for g in range(NG):
                    last = tp(bank[:, tb, P * g:P * g + P], b_raw[:, tb, P * g:P * g + P], ident)
                last.then_inc(cT_ps, 1)
            tp(bank[:, 2, 0:CB], b_pos[0:CB, :], ident[0:CB, 0:CB]).then_inc(pos_ps, 1)
            pe.wait_ge(cin_ready, 1)
            pe.wait_ge(kT_ready, 2)
            arrived(I_CMP)
            arrived(I_CMP + 1)
            for kv in range(2):
                ps = slice(DH * kv, DH * kv + DH)
                for half in range(2):
                    for j in range(CB):
                        w = slot(I_CMP + j // 16).rearrange("p (j c) -> p j c", j=16)
                        last = mm(bank[:, 4 + kv, 64 * half:64 * half + 60], w[ps, j % 16, P * half:P * half + P],
                                  b_cin[ps, j, :, :], start=j == 0, stop=j == CB - 1)
                last.then_inc(hid_ps, 1)
            pe.wait_ge(kT_ready, 4)
            for kv in range(2):
                pe.wait_ge(hid_ready, kv + 1)
                for half in range(2):
                    last = mm(bank[:, 6, DH * kv:DH * kv + DH], b_hid[:, kv, half, :], b_w2[:, kv, half, :],
                              start=half == 0, stop=half == 1)
                last.then_inc(kvc_ps, 1)
            for tb in range(TB):
                for k in range(KD):
                    last = mm(bank[:, 7, 64 * tb:64 * tb + 48], xT[:, k, P * tb:P * tb + P], b_wg[:, k, :],
                              start=k == 0, stop=k == KD - 1)
                last.then_inc(gate_ps, 1)
            pe.wait_ge(pos_ready, 1)
            for j in range(4):
                it, tb = divmod(j, 2)
                if tb == 0:
                    arrived(I_Q + it)
                for k in range(KD):
                    last = mm(bank[:, j, :], xT[:, k, P * tb:P * tb + P], cols(I_Q + it)[:, k, :],
                              start=k == 0, stop=k == KD - 1)
                last.then_inc(q_ps, 1)
            pe.wait_ge(kca_ready, 1)
            tp(bank[0:DA, 5, 0:P], b_kca, ident).then_inc(kcT_ps, 1)
            pe.wait_ge(kcT_ready, 1)
            pe.wait_ge(gate_exp, 2)
            for j in range(4):
                pe.wait_ge(qa_ready, j + 1)
                for a in range(2):
                    n = 2 * j + a
                    if n >= 4:
                        pe.wait_ge(qT_ready, n - 3)
                    for hh in range(4):
                        last = tp(bank[0:DA, 4 + n % 4, P * hh:P * hh + P], b_aug[:, j % 2, 4 * a + hh, :], ident)
                    last.then_inc(qT_ps, 1)
            pe.wait_ge(qT_ready, 8)
            for tb in range(TB):
                for j in range(GRP):
                    for g in range(NG):
                        last = mm(bank[:, tb, 32 * (NG * j + g):32 * (NG * j + g) + 32],
                                  b_qT[0:DA, GRP * g + j, P * tb:P * tb + P], b_kc[0:DA, 32 * g:32 * g + 32],
                                  start=True, stop=True)
                last.then_inc(cs_ps, 1)
            for tb in range(TB):
                pe.wait_ge(cp_ready, tb + 1)
                for j in range(GRP):
                    last = tp(bank[:, 2 + tb, P * j:P * j + P],
                              b_cp[:, NG * j:NG * j + NG, :].rearrange("p g c -> p (g c)"), ident)
                last.then_inc(cpT_ps, 1)
            for tb in range(TB):
                pe.wait_ge(cpT_ready, tb + 1)
                for g in range(NG):
                    ps = slice(32 * g, 32 * g + NCMP)
                    for j in range(GRP):
                        at = 256 * tb + DH * j
                        last = mm(bank[:, 4 + g, at:at + DH], b_cpT[ps, tb, j, :], b_vc[ps, :],
                                  start=True, stop=True)
                    last.then_inc(co_ps, 1)
            pe.wait_ge(co_taken, 4)

            def scores(u):
                br, g, tb = u // 8, u // 2 % 4, u % 2
                if u >= 2:
                    pe.wait_ge(p_ready, u - 1)
                for j in range(GRP):
                    if tb == 0:
                        dst = bank[:, 0, P * j:P * j + P]
                    else:
                        dst = bank[:, 1 + j // 2, T * (j % 2):T * (j % 2) + T]
                    for kb in range(tb + 1):
                        mm(dst[:, P * kb:P * kb + P], b_qT[0:DA, GRP * g + j, P * tb:P * tb + P],
                           b_kT[0:DA, br, g, P * kb:P * kb + P], start=True, stop=kb < tb)
                    last = mm(dst[:, P * tb:P * tb + P], cb[:, 0:P], cb[:, P:2 * P], start=False, stop=True)
                last.then_inc(s_ps, 1)

            def attend(u):
                br, g, tb = u // 8, u // 2 % 4, u % 2
                pe.wait_ge(p_ready, u + 1)
                if u >= 2:
                    pe.wait_ge(pT_ready, u - 1)
                for j in range(GRP):
                    for kb in range(tb + 1):
                        n = (tb + 1) * j + kb
                        b = 3 if tb == 0 else 4 + n // 4
                        last = tp(bank[:, b, P * (n % 4):P * (n % 4) + P], b_p[:, tb, j, P * kb:P * kb + P], ident)
                last.then_inc(pT_ps, 1)
                pe.wait_ge(pT_ready, u + 1)
                if u >= 2:
                    pe.wait_ge(av_taken, u - 1)
                for j in range(GRP):
                    dst = bank[:, 6 + u % 2, DH * j:DH * j + DH]
                    for kb in range(tb + 1):
                        last = mm(dst, b_pT[:, tb, (tb + 1) * j + kb, :], b_v[:, br, kb, DH * g:DH * g + DH],
                                  start=kb == 0, stop=kb == tb)
                last.then_inc(av_ps, 1)

            for u in range(17):
                if u < 16:
                    scores(u)
                if u:
                    attend(u - 1)
            pe.wait_ge(o_added, 16)
            transposed(b_o, bo_ps)
            pe.wait_ge(bo_dve, 1)
            pe.wait_ge(bo_act, 1)
            out_product(I_OUT, xT, 4)
            pe.wait_ge(h_ready, 12)
            norm(3)
            pe.wait_ge(xT_dve, 5)
            pe.wait_ge(xT_act, 4)
            pe.wait_ge(wr_in, 16)
            for tb in range(TB):
                for k in range(KD):
                    last = mm(bank[:, 4, 8 * tb:8 * tb + 8], xT[:, k, P * tb:P * tb + P], m_wr[:, k, :],
                              start=k == 0, stop=k == KD - 1)
                last.then_inc(lg_ps, 1)
            pe.wait_ge(sel_ready, 2)
            tri, ones = cf[:, C_TRI:C_TRI + P], cf[:, C_ONE:C_ONE + 1].broadcast_to([P, P])
            mm(bank[:, 5, 0:8], tri, m_sel[:, 0, :], start=True, stop=True)
            mm(bank[:, 5, 8:16], ones, m_sel[:, 0, :], start=True, stop=False)
            mm(bank[:, 5, 8:16], tri, m_sel[:, 1, :], start=False, stop=True)
            mm(bank[:, 5, 16:24], ones, m_sel[:, 0, :], start=True, stop=False)
            mm(bank[:, 5, 16:24], ones, m_sel[:, 1, :], start=False, stop=True).then_inc(rank_ps, 1)
            pe.wait_ge(route_ready, 2)

            def experts(e, E):
                pe.wait_ge(P_ready, E + 1)
                pe.wait_ge(e_hT, E * NCH + 1)
                for half in range(2):
                    for k in range(4):
                        kk = 4 * half + k
                        for tb in range(TB):
                            last = mm(bank[:, 7 if half == 0 else 4, P * k:P * k + P], xs[:, tb, P * kk:P * kk + P],
                                      m_P[:, tb, :], start=tb == 0, stop=tb == 1)
                    last.then_inc(x_ps, 1)
                for tb in range(TB):
                    last = tp(bank[:, 5, P * tb:P * tb + P], m_PW[:, tb, :], ident)
                last.then_inc(PT_ps, 1)
                pe.wait_ge(mx_act, E + 1)
                pe.wait_ge(mx_dve, E + 1)
                for c in range(NCH + 1):
                    if c < NCH:
                        for half in range(2):
                            at = I_MOE + gu_item(c, half)
                            w = ring[:, at % SLOTS, :].rearrange("p (k c) -> p k c", k=KD)
                            pe.wait_ge(slot_full[at % SLOTS], E * 96 + full(at))
                            b = 2 * (c % 2) + half
                            if c >= 2:
                                pe.wait_ge(e_h, E * NCH + c - 1)
                            else:
                                pe.wait_ge(sc_taken, E * 4 + 1)
                            for k in range(KD):
                                last = mm(bank[:, b, :], m_x[:, k, :], w[:, k, :], start=k == 0, stop=k == KD - 1)
                            last.then_inc(e_gu, 1)
                    if c:
                        pe.wait_ge(e_h, E * NCH + c)
                        pe.wait_ge(e_hT, E * NCH + c)
                        for b in range(4):
                            last = tp(bank[:, 4, P * b:P * b + P], m_h[:, (c - 1) % 2, P * b:P * b + P], ident)
                        last.then_inc(e_hT_ps, 1)
                        pe.wait_ge(e_hT, E * NCH + (c + 1))
                        if c == 1:
                            pe.wait_ge(PT_ready, E + 1)
                        at = I_MOE + down_item(c - 1)
                        w = ring[:, at % SLOTS, :].rearrange("p (b c) -> p b c", b=4)
                        pe.wait_ge(slot_full[at % SLOTS], E * 96 + full(at))
                        for b in range(4):
                            for half in range(2):
                                last = mm(bank[:, 5 + half, :], m_hT[:, (c - 1) % 2, b, :], w[:, b, 512 * half:512 * half + 512],
                                          start=c == 1 and b == 0, stop=c == NCH and b == 3)
                        last.then_inc(e_down, 1)
                pe.wait_ge(y_dve, E + 1)
                pe.wait_ge(y_act, E + 1)
                for j in range(4):
                    tb, half = divmod(j, 2)
                    mm(bank[:, j, :], m_PT[:, P * tb:P * tb + P], m_y[:, 512 * half:512 * half + 512],
                       start=True, stop=True).then_inc(sc_ps, 1)

            with pe.Fori(0, NE) as e:
                experts(e, e)
            pe.wait_ge(route_ready, 3)
            most = pe.value_load(flag[0:1, 0:1], min_val=0, max_val=T)
            with pe.If(most > P):
                with pe.Fori(0, NE) as e:
                    experts(e, e + NE)


_INS = ["x", "norm_mix", "norm_ffn", "hgrn_w_in", "hgrn_w_out", "hgrn_g_norm", "kv_norm", "kv_w",
        "cmp_pos_k", "cmp_w1_k", "cmp_w2_k", "cmp_pos_v", "cmp_w1_v", "cmp_w2_v", "k_norm",
        "nsa_w_in", "nsa_w_out", "nsa_q_norm", "ffn_w_gu", "ffn_w_down", "moe_router", "moe_w_gu",
        "moe_w_down"]


def kernel(**inputs):
    import concourse.bacc as bacc
    from concourse.bass_utils import run_bass_kernel_spmd

    nc = bacc.Bacc("TRN2", target_bir_lowering=False, num_devices=1)
    arrays, args = {}, []
    for name in _INS:
        arrays[f"in_{name}"] = np.ascontiguousarray(inputs[name])
    for name, a in zip(("const_f32", "const_masks"), constants()):
        arrays[f"in_{name}"] = a
    for name, a in arrays.items():
        args.append(nc.dram_tensor(name, a.shape, mybir.dt.from_np(a.dtype), kind="ExternalInput").ap())
    args.append(nc.dram_tensor("out_h", (1, T, D), F32, kind="ExternalOutput").ap())
    trunk(nc, *args)
    result = run_bass_kernel_spmd(nc, [arrays], core_ids=[0])
    return result.results[0]["out_h"]
```

```python
from contextlib import ExitStack

import concourse.bass as bass
import numpy as np
from concourse import mybir

F32 = mybir.dt.float32
F32R = mybir.dt.float32r
BF16 = mybir.dt.bfloat16
U8 = mybir.dt.uint8
I32 = mybir.dt.int32
ALU = mybir.AluOpType
ACT = mybir.ActivationFunctionType
AX = mybir.AxisListType

P = 128
T, D = 256, 1024
TB, KD = T // P, D // P
NH_A, DH_A = 8, 128
NH, NG, GRP, DH = 16, 4, 4, 64
DA = DH + 2
FF, FFE, NE = 2816, 3584, 8
CB, CS, NCMP, CH = 32, 16, 15, 256
EPS, TINY, NEG = 1e-6, 1e-30, -1e30

SLOTS = 7
ARENA = 16384
ITEM = 4096
N_HGRN_IN, N_HGRN_OUT, N_GU, N_DOWN, N_KV, N_CMP, N_Q, N_OUT = 8, 2, 11, 6, 3, 2, 2, 2
I_HOUT = N_HGRN_IN
I_GU = I_HOUT + N_HGRN_OUT
I_DOWN = I_GU + N_GU
I_KV = I_DOWN + N_DOWN
I_CMP = I_KV + N_KV
I_Q = I_CMP + N_CMP
I_OUT = I_Q + N_Q
I_MOE = I_OUT + N_OUT
HALF, RAWS, PARTS = ITEM // 2, 7, 3
NCH = FFE // 512
PER_E = 3 * NCH
HALVES = 2 * PER_E
QUART, F_PARTS = ITEM // 4, 3
N_QUART = 4 * N_GU + FF // P

SCATTER_BANKS = (2, 3, 4, 7)

C_ID, C_IOTA, C_TRI = 0, 128, 256
C_QPOS = 384
C_KPOS = C_QPOS + TB * NH * 2
C_CMASK = C_KPOS + TB * 2
C_CPOS = C_CMASK + TB * 32
C_TIE = C_CPOS + 2
C_HALF = C_TIE + 64
C_ONE = C_HALF + 8
C_ALL = C_ONE + 1

LEVELS = [0, 1, 2, 4, 8, 16, 32, 64, 128]
MLEV = 8

G_MIX0, G_MIX1, G_FFN0, G_FFN1, G_KV, G_HG = 0, 8, 16, 24, 32, 40
R_GAIN = 41
GQ, GK = 0, 1


def constants():
    f = np.zeros((P, C_ALL), np.float32)
    p = np.arange(P)
    f[:, C_ID:C_ID + P] = np.eye(P)
    f[:, C_IOTA:C_IOTA + P] = p
    f[:, C_TRI:C_TRI + P] = p[:, None] < p[None, :]
    f[:, C_ONE] = 1.0
    slope = np.array([2.0 ** (-8.0 * (h + 1) / NH) for h in range(NH)], np.float32)
    for tb in range(TB):
        t = (tb * P + p).astype(np.float32)
        for h in range(NH):
            f[:, C_QPOS + (tb * NH + h) * 2] = -slope[h] * t
            f[:, C_QPOS + (tb * NH + h) * 2 + 1] = slope[h]
        f[:, C_KPOS + tb * 2] = 1.0
        f[:, C_KPOS + tb * 2 + 1] = t
        for c in range(32):
            seen = (t >= c * CS + CB - 1) & (c < NCMP)
            f[:, C_CMASK + tb * 32 + c] = np.where(seen, 0.0, NEG)
    f[:, C_CPOS] = 1.0
    f[:, C_CPOS + 1] = (p % 32) * CS + CB - 1
    f[:, C_TIE:C_TIE + 64] = (np.arange(8)[None, :] < np.arange(8)[:, None]).reshape(1, 64)
    f[:, C_HALF:C_HALF + 8] = -0.5
    m = np.zeros((P, MLEV, P), np.float32)
    s, t = p[:, None], p[None, :]
    for n, lev in enumerate(LEVELS[:MLEV]):
        if lev == 0:
            m[:, n] = s == t
        else:
            m[:, n] = (s // (2 * lev) == t // (2 * lev)) & (s % (2 * lev) < lev) & (t % (2 * lev) >= lev)
    causal = np.where(s >= t, 0.0, NEG)
    return f, np.concatenate([m.reshape(P, MLEV * P), causal], 1).astype(np.float32)


class Steps:

    def __init__(self, eng, sem):
        self.eng, self.sem, self.n, self.loop = eng, sem, 0, None

    def __call__(self, ins):
        self.n += 1
        ins.then_inc(self.sem, 1)
        self.eng.wait_ge(self.sem, self.n if self.loop is None else self.loop + self.n)


def trunk(nc, x, norm_mix, norm_ffn, hgrn_w_in, hgrn_w_out, hgrn_g_norm, kv_norm, kv_w,
          cmp_pos_k, cmp_w1_k, cmp_w2_k, cmp_pos_v, cmp_w1_v, cmp_w2_v, k_norm,
          nsa_w_in, nsa_w_out, nsa_q_norm, ffn_w_gu, ffn_w_down, moe_router, moe_w_gu, moe_w_down,
          const_f32, const_masks, out):
    with ExitStack() as ctx:
        def sb(name, shape, dt=F32):
            return ctx.enter_context(nc.sbuf_tensor(name, shape, dt))

        def sem(name):
            return ctx.enter_context(nc.semaphore(name))

        at0 = -(-nc.sbuf_base // 32) * 32
        ring = sb("ring", [P, SLOTS, ITEM])
        h = sb("h", [P, TB, D])
        at_xs = -(-nc.sbuf_base // 32) * 32
        xs = sb("xs", [P, TB, D])
        at_xT = -(-nc.sbuf_base // 32) * 32
        xT = sb("xT", [P, KD, T])
        cf = sb("cf", [P, C_ALL])
        cu = sb("cu", [P, MLEV, P], U8)
        cb = sb("cb", [P, 3 * P], BF16)
        gain = sb("gain", [P, 48])
        gnar = sb("gnar", [P, 4])
        small = sb("small", [P, 512])
        at_arena = -(-nc.sbuf_base // 32) * 32
        arena = sb("arena", [P, ARENA])
        bank = ctx.enter_context(nc.psum_tensor("bank", [P, 8, 512], F32))

        class Area:

            def __init__(self, at=0):
                self.at = at

            def __call__(self, *dims):
                n = int(np.prod(dims))
                v = arena[:, self.at:self.at + n]
                self.at += n
                assert self.at <= ARENA, self.at
                if len(dims) == 1:
                    return v
                names = "abcd"[:len(dims)]
                kw = {names[i]: dims[i] for i in range(1, len(dims))}
                return v.rearrange(f"p ({' '.join(names)}) -> p {' '.join(names)}", **kw)

        def over(name, shape, at):
            return nc.alloc_sbuf_tensor_at(name, shape, F32R, offset=at)

        raw = ring[:, 1:5, :].rearrange("p s n -> p (s n)")[:, 0:RAWS * HALF].rearrange("p (s n) -> p s n", s=RAWS)
        w_hi = [over(f"w_hi{n}", [P, HALF], at0 + 4 * (ITEM + (RAWS + n) * HALF)) for n in range(PARTS)]
        w_lo = [over(f"w_lo{n}", [P, HALF], at0 + 4 * (ITEM * 6 + n * HALF if n < 2 else 0)) for n in range(PARTS)]
        x_hi, x_lo = (over(f"x_{n}", [P, KD, P], at_xT + 4 * i * KD * P) for i, n in enumerate(("hi", "lo")))
        t_hi, t_lo = (over(f"t_{n}", [P, 2, 4, P], at_arena + 4 * (ARENA - 2048 + 1024 * i)) for i, n in enumerate(("hi", "lo")))

        ring_lo = [over(f"ring_lo{n}", [P, ITEM], at0 + 4 * n * ITEM) for n in range(SLOTS)]
        f_xhi, f_xlo = over("f_xhi", [P, KD, T], at_xs), over("f_xlo", [P, KD, T], at_xT)
        f_hlo, f_hhi = over("f_hlo", [P, 2 * N_GU, T], at_arena), over("f_hhi", [P, 2 * N_GU, T], at_arena + 4 * (2 * N_GU * T + 2048))
        f_whi = [over(f"f_whi{n}", [P, QUART], at_arena + 4 * (ARENA - (n + 1) * QUART)) for n in range(F_PARTS)]
        assert 4 * N_GU * T + 2048 + F_PARTS * QUART <= ARENA

        ident = cf[:, C_ID:C_ID + P]

        A = Area()
        a_q, a_k, a_c = A(NH_A, T), A(NH_A, T), A(NH_A, T)
        a_x, a_ql, a_kl = A(NH_A, T), A(NH_A, T), A(NH_A, T)
        a_st = A(2, TB, 4, P)
        a_v = A(TB, D)
        a_so = xT[:, 0:4, :].rearrange("p k t -> p (k t)").rearrange("p (g j t) -> p g j t", g=2, j=4)
        a_sg = xs
        a_oT = arena[:, 4 * 2048:5 * 2048].rearrange("p (k t) -> p k t", k=KD)
        a_on = arena[:, 3 * 2048:4 * 2048].rearrange("p (b n) -> p b n", b=TB)
        a_sq = arena[:, 5 * 2048:6 * 2048].rearrange("p (b n) -> p b n", b=4)
        A = Area(2 * N_GU * T)
        f_sl = A(4, 256)
        f_hm = A(2, TB, 256)
        A = Area()
        b_xk = A(KD, T)
        b_qT = A(NH, T)
        b_kT = A(2, NG, T)
        b_v = A(2, TB, NG * DH)
        b_kc = A(P)
        b_vc = A(DH)
        b_o = A(TB, D)
        b_cin = b_o.rearrange("p b n -> p (b n)")[:, 0:CB * NG * NCMP].rearrange("p (j g c) -> p j g c", g=NG, c=NCMP)
        b_gate = A(TB, 48)
        U = A.at
        b_aug = A(2, 8, DA)
        b_sq = A(512)
        b_cT = A(NG, T)
        b_raw = xs
        b_w2 = A(2, 2, DH)
        b_pos = A(P)
        b_posT = A(CB)
        b_hid = A(2, 2, P)
        b_hs = b_cT.rearrange("p g t -> p (g t)")[:, 0:2 * CH].rearrange("p (k c) -> p k c", k=2)
        b_kca = A(DA)
        b_wg = A(KD, 48)
        A = Area(U)
        b_p = A(2, 4, T)
        b_pT = A(2, 8, P)
        b_t = arena[:, 0:256]
        b_cp = A(NH, 32)
        b_cpT = b_pT
        A = Area()
        m_sel, m_pos, m_wt = A(TB, NE + 1), A(2 * TB, NE + 1), A(TB, NE + 1)
        m_cmp = A(NE, NE)
        m_cmp2 = A(NE, NE)
        m_lg = A(TB, NE)
        m_wr = A(KD, NE)
        m_P = A(TB, P)
        m_PW = A(TB, P)
        m_PT = A(T)
        m_sl = A(2, 512)
        m_h = A(2, 512)
        m_y = A(D)
        flag = sb("flag", [P, 1], I32)

        slot_full = [sem(f"slot_full{s}") for s in range(SLOTS)]
        q_used, q_hi, q_lo, f_x_ok, f_h_ok = (sem(n) for n in ("q_used", "q_hi", "q_lo", "f_x_ok", "f_h_ok"))
        x_in, const_in, gain_in, misc_in, wr_in = (sem(n) for n in ("x_in", "const_in", "gain_in", "misc_in", "wr_in"))
        gains_ps, gains_ok = sem("gains_ps"), sem("gains_ok")
        h_ready = sem("h_ready")
        ss_ready, rs_ready, xs_ready = sem("ss_ready"), sem("rs_ready"), sem("xs_ready")
        xT_ps, xT_dve, xT_act = sem("xT_ps"), sem("xT_dve"), sem("xT_act")
        proj_ready, f_logged, f_taken, key_ok, qv_taken = (
            sem(n) for n in ("proj_ready", "f_logged", "f_taken", "key_ok", "qv_taken"))
        dist_ready, fac_ready, ops_ready, pair_ps, pair_taken, zeroed = (
            sem(n) for n in ("dist_ready", "fac_ready", "ops_ready", "pair_ps", "pair_taken", "zeroed"))
        o_ps, osq_ready, oss_ready, ors_ready, on_ready, oT_ps, oT_dve, oT_act = (
            sem(n) for n in ("o_ps", "osq_ready", "oss_ready", "ors_ready", "on_ready", "oT_ps", "oT_dve", "oT_act"))
        sg_ready, res_ps = sem("sg_ready"), sem("res_ps")
        gu_ps, sl_ready, hm_ready, hT_ps, hT_ready = (
            sem(n) for n in ("gu_ps", "sl_ready", "hm_ready", "hT_ps", "hT_ready"))
        o_added, kv_ps, kv_sq, kv_ss, kv_rs, kv_norm_ok, kv_raw, kv_v = (
            sem(n) for n in ("o_added", "kv_ps", "kv_sq", "kv_ss", "kv_rs", "kv_norm_ok", "kv_raw", "kv_v"))
        kT_ps, kT_ready, cT_ps, cT_ready, cin_ready, hid_ps, hs_ready, hsT_ps, hid_ready, kvc_ps, kvc_ready, kc_sq = (
            sem(n) for n in ("kT_ps", "kT_ready", "cT_ps", "cT_ready", "cin_ready", "hid_ps", "hs_ready", "hsT_ps", "hid_ready", "kvc_ps", "kvc_ready", "kc_sq"))
        kc_ss, kc_rs, kca_ready, kcT_ps, kcT_ready, pos_ps, pos_ready = (
            sem(n) for n in ("kc_ss", "kc_rs", "kca_ready", "kcT_ps", "kcT_ready", "pos_ps", "pos_ready"))
        gate_ps, gate_exp, gate_ready = sem("gate_ps"), sem("gate_exp"), sem("gate_ready")
        q_ps, q_sq, q_ss, q_rs, qa_ready, qT_ps, qT_ready = (
            sem(n) for n in ("q_ps", "q_sq", "q_ss", "q_rs", "qa_ready", "qT_ps", "qT_ready"))
        cs_ps, cs_shift, cs_exp, cp_ready, cpT_ps, cpT_ready, co_ps, co_taken = (
            sem(n) for n in ("cs_ps", "cs_shift", "cs_exp", "cp_ready", "cpT_ps", "cpT_ready", "co_ps", "co_taken"))
        s_ps, max_ready, p_ready, pT_ps, pT_ready, av_ps, av_taken = (
            sem(n) for n in ("s_ps", "max_ready", "p_ready", "pT_ps", "pT_ready", "av_ps", "av_taken"))
        bo_ps, bo_dve, bo_act = sem("bo_ps"), sem("bo_dve"), sem("bo_act")
        lg_ps, lg_shift, lg_exp, sel_ready, rank_ps, route_ready = (
            sem(n) for n in ("lg_ps", "lg_shift", "lg_exp", "sel_ready", "rank_ps", "route_ready"))
        raw_full = [sem(f"raw_full{n}") for n in range(RAWS)]
        hi_ready, lo_ready, w_free = sem("hi_ready"), sem("lo_ready"), sem("w_free")
        P_made, P_ready, x_ps, x_hi_ok, x_lo_ok, PT_ps, PT_ready = (
            sem(n) for n in ("P_made", "P_ready", "x_ps", "x_hi_ok", "x_lo_ok", "PT_ps", "PT_ready"))
        e_sl, e_h, e_hT_ps, t_hi_ok, t_lo_ok, y_ready, sc_ps, sc_taken = (
            sem(n) for n in ("e_sl", "e_h", "e_hT_ps", "t_hi_ok", "t_lo_ok", "y_ready", "sc_ps", "sc_taken"))
        out_done = sem("out_done")
        dve_step, act_step, pool_step, dve_loop = sem("dve_step"), sem("act_step"), sem("pool_step"), sem("dve_loop")
        init_ok, masks_ok = sem("init_ok"), sem("masks_ok")
        S_SS, S_MS, S_RS = 0, 8, 16
        S_O = 32
        S_K = 96
        S_Q = 160
        S_C = 272
        S_CM = 288
        S_A = 400
        S_L = 440

        block = ctx.enter_context(nc.Block())

        def slot(i):
            return ring[:, i % SLOTS, :]

        def halves(v, m):
            return v.rearrange("p n t -> p (n t)").rearrange("p (b w m) -> p b w m", w=2, m=m)

        def full(i):
            return 32 * (i // SLOTS + 1)

        def quarter_used(d):
            n, a = divmod(d, 4)
            if n < N_GU:
                return (gu_ps, 2 * n + 2) if a == 3 else (q_used, 3 * n + a + 1)
            return q_used, 3 * N_GU + d - 4 * N_GU + 1

        def quarter(d):
            s, a = (I_GU + d // 4) % SLOTS, slice(QUART * (d % 4), QUART * (d % 4) + QUART)
            return ring[:, s, a], ring_lo[s][:, a]

        def left(i):
            if i < I_HOUT:
                return proj_ready, 2 * i + 2
            if i < I_GU:
                return res_ps, 2 * (i - I_HOUT) + 2
            if i < I_DOWN:
                return gu_ps, 2 * (i - I_GU) + 2
            if i < I_KV - 1:
                return quarter_used(4 * (i - I_GU) + 3)
            if i < I_KV:
                return res_ps, 8
            if i < I_CMP:
                return kv_ps, 2 * (i - I_KV) + 2
            if i < I_Q:
                return hid_ps, 2
            if i < I_OUT:
                return q_ps, 2 * (i - I_Q) + 2
            return res_ps, 8 + 2 * (i - I_OUT) + 2

        def gu_item(c, half):
            return half if c == 0 else 3 * c - 1 + half

        def down_item(c):
            return 3 * c + 4 if c < NCH - 1 else PER_E - 1

        expert_items = sorted([(gu_item(c, g), "gate up".split()[g], c) for c in range(NCH) for g in range(2)]
                              + [(down_item(c), "down", c) for c in range(NCH)])

        def used(s, E):
            return w_free, E * HALVES + (s + 1 + PARTS)

        def part_of(s, w):
            return w[s % PARTS][:, :].rearrange("p (k c) -> p k c", c=D if expert_items[s // 2][1] == "down" else 512)

        def split_part(eng, s, E):
            if s >= HALVES:
                s, E = s - HALVES, E + 1
            eng.wait_ge(w_free, E * HALVES + (s + 1))
            eng.wait_ge(raw_full[s % RAWS], E * (16 * HALVES // RAWS) + 16 * (s // RAWS + 1))
            return s, E

        @block.sync
        def _(sp):
            sp.dma_start(h[:, 0, :], x[0, 0:P, :]).then_inc(x_in, 16)
            sp.dma_start(h[:, 1, :], x[0, P:T, :]).then_inc(x_in, 16)
            g = arena[:, 0:128]
            for k, (w, r) in enumerate(((norm_mix, G_MIX0), (norm_ffn, G_FFN0))):
                sp.dma_start(g[r:r + 16, :], w.rearrange("l (k p) -> (l k) p", p=P)).then_inc(gain_in, 16)
            sp.dma_start(g[G_KV:G_KV + 8, :], kv_norm.rearrange("(k p) -> k p", p=P)).then_inc(gain_in, 16)
            sp.dma_start(g[G_HG:G_HG + 1, :], hgrn_g_norm).then_inc(gain_in, 16)
            sp.dma_start(arena[GQ:GQ + 1, 128:128 + DH], nsa_q_norm).then_inc(gain_in, 16)
            sp.dma_start(arena[GK:GK + 3, 128:128 + DH], k_norm).then_inc(gain_in, 16)
            i = 0

            def load(parts):
                nonlocal i
                if i >= SLOTS:
                    sp.wait_ge(*left(i - SLOTS))
                for dst, src in parts:
                    sp.dma_start(dst, src).then_inc(slot_full[i % SLOTS], 16)
                i += 1

            def columns(w, c0):
                dst = slot(i).rearrange("p (k c) -> p k c", k=KD)
                src = w[:, c0:c0 + 512].rearrange("(k p) c -> p k c", p=P)
                return [(dst[:, 4 * a:4 * a + 4, :], src[:, 4 * a:4 * a + 4, :]) for a in range(2)]

            w = hgrn_w_in[0]
            for part in (1, 0, 2, 3):
                for c in range(2):
                    load(columns(w, part * D + c * 512))
            for c in range(2):
                load(columns(hgrn_w_out[0], c * 512))
            for n in range(N_GU):
                dst = slot(i).rearrange("p (k g c) -> p k g c", k=KD, g=2)
                load([(dst[:, :, g, :], ffn_w_gu[0, :, g * FF + n * 256:g * FF + (n + 1) * 256]
                       .rearrange("(k p) c -> p k c", p=P)) for g in range(2)])
            for n in range(N_DOWN):
                b = min(4, FF // P - 4 * n)
                dst = slot(i).rearrange("p (b c) -> p b c", b=4)
                src = ffn_w_down[0, 4 * n * P:(4 * n + b) * P, :].rearrange("(b p) c -> p b c", p=P)
                load([(dst[:, 0:b, 512 * a:512 * a + 512], src[:, :, 512 * a:512 * a + 512]) for a in range(2)])
            for c in range(N_KV):
                load(columns(kv_w, c * 512))
            for a in range(N_CMP):
                dst = slot(i).rearrange("p (j c) -> p j c", j=16)
                load([(dst[DH * kv:DH * kv + DH, :, :],
                       w1[a * 16 * DH:(a + 1) * 16 * DH, :].rearrange("(j d) c -> d j c", d=DH))
                      for kv, w1 in enumerate((cmp_w1_k, cmp_w1_v))])
            for c in range(N_Q):
                load(columns(nsa_w_in[0], c * 512))
            for c in range(N_OUT):
                load(columns(nsa_w_out[0], c * 512))
            assert i == I_MOE

            def halves_of(e, E, first, last):
                for s in range(first, last):
                    (_, kind, c), a = expert_items[s // 2], s % 2
                    if not (isinstance(E, int) and HALVES * E + s < RAWS):
                        sp.wait_ge(lo_ready, E * HALVES + (s - RAWS + 1))
                    if kind == "down":
                        src = moe_w_down[0, bass.ds(e, 1), c * 512 + a * 256:c * 512 + (a + 1) * 256, :]
                    else:
                        c0 = (kind == "up") * FFE + c * 512
                        src = moe_w_gu[0, bass.ds(e, 1), 512 * a:512 * a + 512, c0:c0 + 512]
                    src = src.rearrange("o (k p) c -> p (o k) c", p=P)
                    dst = raw[:, s % RAWS, :].rearrange("p (k c) -> p k c", c=D if kind == "down" else 512)
                    sp.dma_start(dst, src).then_inc(raw_full[s % RAWS], 16)

            def all_experts(first, E0):
                halves_of(0, E0, first, RAWS)
                with sp.Fori(0, NE - 1) as e:
                    halves_of(e, e + E0, RAWS, HALVES)
                    halves_of(e + 1, e + (E0 + 1), 0, RAWS)
                halves_of(NE - 1, E0 + NE - 1, RAWS, HALVES)
                halves_of(0, E0 + NE, 0, PARTS - 1)

            sp.wait_ge(*left(I_Q))
            all_experts(0, 0)
            sp.wait_ge(route_ready, 3)
            most = sp.value_load(flag[0:1, 0:1], min_val=0, max_val=T)
            with sp.If(most > P):
                all_experts(PARTS - 1, NE)

        @block.gpsimd
        def _(pool):
            step = Steps(pool, pool_step)
            pool.dma_start(cf[:], const_f32).then_inc(const_in, 16)
            masks = arena[:, 2048:2048 + (MLEV + 1) * P]
            pool.dma_start(masks, const_masks).then_inc(const_in, 16)
            pool.wait_ge(const_in, 32)

            def inverse_rms(sums, n, width, got, count, told):
                pool.wait_ge(got, count)
                mean = small[:, sums + n:sums + 2 * n]
                step(pool.tensor_scalar(mean, small[:, sums:sums + n], 1.0 / width, EPS, ALU.mult, ALU.add))
                pool.tensor_tensor(small[:, sums + 2 * n:sums + 3 * n], mean,
                                   cf[:, C_HALF:C_HALF + n], ALU.pow).then_inc(told, 1)

            def norm(i):
                for tb in range(TB):
                    inverse_rms(S_SS + 3 * (2 * i + tb), 1, D, ss_ready, 2 * i + tb + 1, rs_ready)

            norm(0)
            pool.tensor_copy(cu[:].rearrange("p m t -> p (m t)"), masks[:, 0:MLEV * P]).then_inc(masks_ok, 1)
            pool.tensor_copy(cb[:, 0:P], cf[:, C_ID:C_ID + P]).then_inc(masks_ok, 1)
            pool.memset(cb[:, P:2 * P], 0.0).then_inc(masks_ok, 1)
            pool.tensor_copy(cb[:, 2 * P:3 * P], masks[:, MLEV * P:]).then_inc(masks_ok, 1)
            pool.memset(a_st, 0.0).then_inc(zeroed, 1)
            pool.memset(a_ql, 0.0)
            pool.memset(a_kl, 0.0).then_inc(zeroed, 1)
            for j in range(4):
                inverse_rms(S_O + 12 * j, 4, DH_A, oss_ready, j + 1, ors_ready)
            norm(1)
            norm(2)
            for j in range(4):
                inverse_rms(S_K + 12 * j, 4, DH, kv_ss, j + 1, kv_rs)
            inverse_rms(S_C, 1, DH, kc_ss, 1, kc_rs)
            for j in range(4):
                inverse_rms(S_Q + 24 * j, 8, DH, q_ss, j + 1, q_rs)
            norm(3)

        @block.scalar
        def _(act):
            step = Steps(act, act_step)
            def norm(i, h_count):
                for tb in range(TB):
                    if i == 0:
                        act.wait_ge(x_in, 32)
                    else:
                        act.wait_ge(h_ready, h_count[tb])
                    act.activation(xs[:, tb, :], h[:, tb, :], ACT.Square,
                                   accum_out=small[:, S_SS + 3 * (2 * i + tb):S_SS + 3 * (2 * i + tb) + 1]
                                   ).then_inc(ss_ready, 1)

            def transposed(i, g0):
                for b in (1, 3):
                    act.wait_ge(xT_ps, 4 * i + b + 1)
                    for k in (2 * b, 2 * b + 1):
                        last = act.activation(xT[:, k, :], bank[:, b, 256 * (k % 2):256 * (k % 2) + 256],
                                              ACT.Copy, scale=gain[:, g0 + k:g0 + k + 1])
                last.then_inc(xT_act, 1)

            norm(0, None)
            act.wait_ge(gains_ok, 1)
            transposed(0, G_MIX0)
            for j in range(4):
                cc, xx = a_c[:, 2 * j:2 * j + 2, :], a_x[:, 2 * j:2 * j + 2, :]
                act.wait_ge(proj_ready, j + 1)
                step(act.activation(xx, bank[:, j, :], ACT.Abs))
                step(act.activation(xx, xx, ACT.Exp, scale=-1.0))
                act.activation(xx, xx, ACT.Ln, bias=1.0).then_inc(f_logged, 1)
            for j in range(4):
                kk = a_k[:, 2 * j:2 * j + 2, :]
                act.wait_ge(f_taken, j + 1)
                act.activation(kk, kk, ACT.Exp).then_inc(key_ok, 1)
            for j in range(4):
                act.wait_ge(proj_ready, 5 + j)
                act.activation(a_q[:, 2 * j:2 * j + 2, :], bank[:, j, :], ACT.Silu).then_inc(qv_taken, 1)
            act.wait_ge(xs_ready, 2)
            act.wait_ge(xT_ps, 4)
            u = 0
            for n in range(9):
                if n >= 1:
                    for grp in range(2):
                        m = LEVELS[n]
                        hs = slice(4 * grp, 4 * grp + 4)
                        cR = halves(a_c[:, hs, :], m)[:, :, 1, :]
                        xR = halves(a_x[:, hs, :], m)[:, :, 1, :]
                        xL = halves(a_x[:, hs, :], m)[:, :, 0, :]
                        u += 1
                        if m > 1:
                            act.wait_ge(dist_ready, u - 2)
                        last = act.activation(xR, cR, ACT.Exp)
                        if m > 1:
                            last = act.activation(xL, xL, ACT.Exp)
                        last.then_inc(fac_ready, 1)
                if n < 8:
                    act.wait_ge(proj_ready, 9 + n)
                    it, tb = divmod(n % 4, 2)
                    dst = (a_v if n < 4 else a_sg)[:, tb, 512 * it:512 * it + 512]
                    act.activation(dst, bank[:, n % 4, :], ACT.Copy).then_inc(qv_taken, 1)
            act.wait_ge(qv_taken, 12)
            act.activation(a_sg[:, :, :], a_sg[:, :, :], ACT.Silu).then_inc(sg_ready, 1)
            for j in range(4):
                act.wait_ge(o_ps, j + 1)
                act.wait_ge(pair_ps, 18)
                act.activation(a_sq[:, j, :], bank[:, j, :], ACT.Square).then_inc(osq_ready, 1)
            for b in (1, 3):
                act.wait_ge(oT_ps, b + 1)
                for k in (2 * b, 2 * b + 1):
                    last = act.activation(a_oT[:, k, :], bank[:, 4 + b, 256 * (k % 2):256 * (k % 2) + 256],
                                          ACT.Copy, scale=gain[:, G_HG:G_HG + 1])
            last.then_inc(oT_act, 1)
            quarters = [0]

            def round_to(n):
                for d in range(quarters[0], min(n, N_QUART)):
                    act.wait_ge(slot_full[(I_GU + d // 4) % SLOTS], full(I_GU + d // 4))
                    if d >= F_PARTS:
                        act.wait_ge(*quarter_used(d - F_PARTS))
                    act.activation(f_whi[d % F_PARTS][:, :], quarter(d)[0], ACT.Copy).then_inc(q_hi, 1)
                quarters[0] = n

            round_to(F_PARTS)
            norm(1, (3, 4))
            act.wait_ge(xT_ps, 8)
            for k in range(KD):
                act.activation(f_xhi[:, k, :], bank[:, k // 2, 256 * (k % 2):256 * (k % 2) + 256],
                               ACT.Copy, scale=gain[:, G_FFN0 + k:G_FFN0 + k + 1]).then_inc(f_x_ok, 1)
            for n in range(N_GU + 1):
                round_to(min(4 * n + 6, 4 * N_GU + F_PARTS))
                if n < N_GU:
                    for j in (2 * n, 2 * n + 1):
                        act.wait_ge(gu_ps, j + 1)
                        if j >= 4:
                            act.wait_ge(hm_ready, j - 3)
                        act.activation(f_sl[:, j % 4, :], bank[:, j % 4, 0:256], ACT.Silu).then_inc(sl_ready, 1)
                if n:
                    act.wait_ge(hT_ps, n)
                    act.activation(f_hhi[:, 2 * n - 2:2 * n, :].rearrange("p b t -> p (b t)"), bank[:, 4 + (n - 1) % 2, :],
                                   ACT.Copy).then_inc(f_h_ok, 1)
            round_to(N_QUART)
            norm(2, (6, 8))
            act.dma_start(b_pos[0:CB, 0:DH], cmp_pos_k).then_inc(misc_in, 16)
            act.dma_start(b_pos[0:CB, DH:2 * DH], cmp_pos_v).then_inc(misc_in, 16)
            for kv, w2 in enumerate((cmp_w2_k, cmp_w2_v)):
                act.dma_start(b_w2[:, kv, :, :], w2.rearrange("(b p) d -> p b d", p=P)).then_inc(misc_in, 16)
            act.dma_start(b_wg, nsa_w_in[0, :, D:D + 48].rearrange("(k p) c -> p k c", p=P)).then_inc(misc_in, 16)
            transposed(2, G_MIX1)
            for j in range(6):
                it, tb = divmod(j, 2)
                act.wait_ge(kv_ps, j + 1)
                if it == 0:
                    act.activation(b_raw[:, tb, 0:512].rearrange("p (g v d) -> p v g d", v=2, g=NG),
                                   bank[:, j % 4, :].rearrange("p (v g d) -> p v g d", v=2, g=NG),
                                   ACT.Copy).then_inc(kv_raw, 1)
                else:
                    if j > 2:
                        act.wait_ge(kv_ss, j - 2)
                    step(act.activation(b_v[:, it - 1, tb, :], bank[:, j % 4, 256:512], ACT.Copy))
                    act.activation(b_sq[:, 0:256], bank[:, j % 4, 0:256], ACT.Square).then_inc(kv_sq, 1)
            for kv in range(2):
                act.wait_ge(hid_ps, kv + 1)
                act.activation(b_hs[0:NG * NCMP, kv, :], bank[0:NG * NCMP, 4 + kv, 0:CH], ACT.Silu).then_inc(hs_ready, 1)
            act.wait_ge(kvc_ps, 2)
            act.wait_ge(kv_ss, 4)
            act.activation(b_sq[:, 0:DH], bank[:, 6, 0:DH], ACT.Square,
                           accum_out=small[:, S_C:S_C + 1]).then_inc(kc_ss, 1)
            act.wait_ge(gate_ps, 2)
            for tb in range(TB):
                act.activation(b_gate[:, tb, :], bank[:, 7, 64 * tb:64 * tb + 48], ACT.Exp, scale=-1.0).then_inc(gate_exp, 1)
            for j in range(4):
                act.wait_ge(q_ps, j + 1)
                act.wait_ge(kc_ss, 1)
                if j:
                    act.wait_ge(q_ss, j)
                act.activation(b_sq[:, :], bank[:, j, :], ACT.Square).then_inc(q_sq, 1)
            for tb in range(TB):
                act.wait_ge(cs_shift, tb + 1)
                act.activation(b_cp[:, :, :], b_cp[:, :, :], ACT.Exp).then_inc(cs_exp, 1)
            for u in range(16):
                tb, n = u % 2, P * (u % 2 + 1)
                act.wait_ge(max_ready, u + 1)
                if u >= 2:
                    act.wait_ge(pT_ps, u - 1)
                st = small[:, S_A + 16 * (u % 2):]
                for j in range(GRP):
                    src = (bank[:, 0, :].rearrange("p (j k) -> p j k", j=4) if tb == 0
                           else bank[:, 1:3, :].rearrange("p b (j k) -> p (b j) k", j=2))[:, j, 0:n]
                    last = act.activation(b_p[:, u % 2, j, 0:n], src, ACT.Exp,
                                          bias=small[:, S_A + 16 * (u % 2) + j:S_A + 16 * (u % 2) + j + 1],
                                          accum_out=small[:, S_A + 16 * (u % 2) + 4 + j:S_A + 16 * (u % 2) + 5 + j])
                last.then_inc(p_ready, 1)
            for b in (1, 3):
                act.wait_ge(bo_ps, b + 1)
                for k in (2 * b, 2 * b + 1):
                    last = act.activation(xT[:, k, :], bank[:, b, 256 * (k % 2):256 * (k % 2) + 256], ACT.Copy)
            last.then_inc(bo_act, 1)
            act.wait_ge(o_added, 16)
            act.dma_start(m_wr, moe_router[0].rearrange("(k p) c -> p k c", p=P)).then_inc(wr_in, 16)
            norm(3, (11, 12))
            transposed(3, G_FFN1)
            for tb in range(TB):
                act.wait_ge(lg_shift, tb + 1)
                act.activation(m_lg[:, tb, :], m_lg[:, tb, :], ACT.Exp).then_inc(lg_exp, 1)

            splits = [0]

            def split_to(n, E):
                for s0 in range(splits[0], n):
                    s, E1 = split_part(act, s0, E)
                    act.activation(w_hi[s % PARTS][:, :], raw[:, s % RAWS, :], ACT.Copy).then_inc(hi_ready, 1)
                splits[0] = n

            def gathered(half, G):
                act.wait_ge(x_ps, G * 2 + (half + 1))
                for k in range(4 * half, 4 * half + 4):
                    last = act.activation(x_hi[:, k, :], bank[:, 7, P * (k % 4):P * (k % 4) + P], ACT.Copy,
                                          scale=gain[:, G_FFN1 + k:G_FFN1 + k + 1])
                last.then_inc(x_hi_ok, 1)

            def hidden(c, E):
                act.wait_ge(e_hT_ps, E * NCH + (c + 1))
                act.activation(t_hi[:, c % 2, :, :], bank[:, 4, :], ACT.Copy).then_inc(t_hi_ok, 1)

            def expert(e, E, q):
                for c in range(NCH):
                    s = 2 * gu_item(c, 0) + 1
                    split_to(s + PARTS, E)
                    act.wait_ge(*used(s, E))
                    if c >= 2:
                        act.wait_ge(e_h, E * NCH + (c - 1))
                    act.activation(m_sl[:, c % 2, :], bank[:, 2 * (c % 2), :], ACT.Silu).then_inc(e_sl, 1)
                    if c:
                        hidden(c - 1, E)
                    if c == 1:
                        split_to(2 * gu_item(1, 1) + 1 + PARTS, E)
                        act.wait_ge(PT_ps, E + 1)
                        act.activation(m_PT[:, :], bank[:, 7, 0:T], ACT.Copy).then_inc(PT_ready, 1)
                split_to(2 * gu_item(NCH - 1, 1) + 1 + PARTS, E)
                gathered(0, E + (1 + q))
                split_to(2 * down_item(NCH - 2) + 1 + PARTS, E)
                hidden(NCH - 1, E)
                gathered(1, E + (1 + q))
                split_to(HALVES - 1 + PARTS, E)
                act.wait_ge(*used(HALVES - 1, E))
                act.activation(m_y[:, :], bank[:, 5:7, :].rearrange("p b n -> p (b n)"), ACT.Copy).then_inc(y_ready, 1)
                splits[0] = PARTS - 1

            def all_experts(E0, q):
                gathered(0, E0 + q)
                gathered(1, E0 + q)
                with act.Fori(0, NE) as e:
                    expert(e, e + E0, q)

            split_to(PARTS - 1, 0)
            all_experts(0, 0)
            act.wait_ge(route_ready, 3)
            most = act.value_load(flag[0:1, 0:1], min_val=0, max_val=T)
            with act.If(most > P):
                all_experts(NE, 1)
            act.wait_ge(h_ready, 13)
            for tb in range(TB):
                act.dma_start(out[0, tb * P:(tb + 1) * P, :], h[:, tb, :]).then_inc(out_done, 16)
            act.wait_ge(out_done, 32)

        @block.vector
        def _(dve):
            step = Steps(dve, dve_step)
            dve.wait_ge(const_in, 32)

            def norm(i):
                for tb in range(TB):
                    dve.wait_ge(rs_ready, 2 * i + tb + 1)
                    dve.tensor_scalar(xs[:, tb, :], h[:, tb, :],
                                      small[:, S_SS + 3 * (2 * i + tb) + 2:S_SS + 3 * (2 * i + tb) + 3],
                                      None, ALU.mult).then_inc(xs_ready, 1)

            def transposed(i, g0, dst=xT, banks=(0, 2), told=xT_dve):
                for b in banks:
                    dve.wait_ge(xT_ps, 4 * i + b + 1)
                    for k in (2 * b, 2 * b + 1):
                        last = dve.tensor_scalar(dst[:, k, :], bank[:, b, 256 * (k % 2):256 * (k % 2) + 256],
                                                 gain[:, g0 + k:g0 + k + 1], None, ALU.mult)
                last.then_inc(told, 1)

            norm(0)
            dve.wait_ge(gain_in, 96)
            dve.memset(arena[0:4, 128 + DH:128 + DA], 1.0).then_inc(gains_ps, 1)
            dve.wait_ge(gains_ps, 2)
            dve.tensor_copy(gain[:, 0:R_GAIN], bank[:, 4, 0:R_GAIN])
            dve.tensor_copy(gnar[0:DA, :], bank[0:DA, 4, 64:68]).then_inc(gains_ok, 1)
            dve.wait_ge(gains_ok, 1)
            step(dve.tensor_scalar(gnar[0:DH, GQ:GQ + 1], gnar[0:DH, GQ:GQ + 1], float(DH) ** -0.5, None, ALU.mult))
            transposed(0, G_MIX0)
            dve.wait_ge(masks_ok, 4)
            for j in range(4):
                cc, xx, kk = (v[:, 2 * j:2 * j + 2, :] for v in (a_c, a_x, a_k))
                dve.wait_ge(f_logged, j + 1)
                step(dve.scalar_tensor_tensor(cc, bank[:, j, :], 0.0, xx, ALU.min, ALU.subtract))
                dve.tensor_tensor(kk, cc, bank[:, j, :], ALU.subtract).then_inc(f_taken, 1)
            dve.wait_ge(zeroed, 2)
            dve.wait_ge(key_ok, 4)
            dve.wait_ge(qv_taken, 4)

            def take_pairs(n, grp):
                for tb in range(TB):
                    dve.wait_ge(pair_ps, 2 * n + grp + 1)
                    b = 4 + 2 * grp + tb
                    if n == MLEV:
                        if tb == 0:
                            dve.tensor_copy(a_so[:, grp, :, :], bank[:, b, :]).then_inc(pair_taken, 1)
                    else:
                        ins = dve.copy_predicated(a_st[:, grp, tb, :, :],
                                                  cu[:, n, :].unsqueeze(1).broadcast_to([P, 4, P]),
                                                  bank[:, b, :].rearrange("p (j t) -> p j t", j=4))
                        if tb:
                            ins.then_inc(pair_taken, 1)

            for n in range(1, 9):
                m = LEVELS[n]
                for grp in range(2):
                    hs = slice(4 * grp, 4 * grp + 4)
                    c_, x_, q_, k_, ql, kl = (halves(v[:, hs, :], m) for v in (a_c, a_x, a_q, a_k, a_ql, a_kl))
                    nb = 1024 // (2 * m)
                    end = c_[:, :, 0, m - 1:m].broadcast_to([P, nb, m])
                    if m > 1:
                        dve.tensor_tensor(x_[:, :, 0, :], end, c_[:, :, 0, :], ALU.subtract).then_inc(dist_ready, 1)
                for grp in range(2):
                    take_pairs(n - 1, grp)
                    hs = slice(4 * grp, 4 * grp + 4)
                    c_, x_, q_, k_, ql, kl = (halves(v[:, hs, :], m) for v in (a_c, a_x, a_q, a_k, a_ql, a_kl))
                    end = c_[:, :, 0, m - 1:m].broadcast_to([P, nb, m])
                    dve.wait_ge(fac_ready, 2 * (n - 1) + grp + 1)
                    last = dve.tensor_tensor(ql[:, :, 1, :], q_[:, :, 1, :], x_[:, :, 1, :], ALU.mult)
                    if m > 1:
                        last = dve.tensor_tensor(kl[:, :, 0, :], k_[:, :, 0, :], x_[:, :, 0, :], ALU.mult)
                    last.then_inc(ops_ready, 1)
                    if n < 8:
                        step(dve.tensor_tensor(c_[:, :, 1, :], c_[:, :, 1, :], end, ALU.add))
            for grp in range(2):
                take_pairs(8, grp)
            for j in range(4):
                tb, grp = divmod(j, 2)
                st = S_O + 12 * j
                dve.wait_ge(osq_ready, j + 1)
                dve.tensor_reduce(small[:, st:st + 4], a_sq[:, j, :].rearrange("p (n d) -> p n d", n=4),
                                  AX.X, ALU.add).then_inc(oss_ready, 1)
                dve.wait_ge(sg_ready, 1)
                dst = a_on[:, tb, 512 * grp:512 * grp + 512]
                step(dve.tensor_tensor(dst, bank[:, j, :], a_sg[:, tb, 512 * grp:512 * grp + 512], ALU.mult))
                dve.wait_ge(ors_ready, j + 1)
                d3 = dst.rearrange("p (n d) -> p n d", n=4)
                dve.tensor_tensor(d3, d3, small[:, st + 8:st + 12].unsqueeze(2).broadcast_to([P, 4, DH_A]),
                                  ALU.mult).then_inc(on_ready, 1)
            for b in (0, 2):
                dve.wait_ge(oT_ps, b + 1)
                for k in (2 * b, 2 * b + 1):
                    last = dve.tensor_scalar(a_oT[:, k, :], bank[:, 4 + b, 256 * (k % 2):256 * (k % 2) + 256],
                                             gain[:, G_HG:G_HG + 1], None, ALU.mult)
            last.then_inc(oT_dve, 1)
            quarters = [0]

            def rest_to(n):
                for d in range(quarters[0], min(n, N_QUART)):
                    dve.wait_ge(q_hi, d + 1)
                    dve.tensor_tensor(quarter(d)[1], quarter(d)[0], f_whi[d % F_PARTS][:, :].bitcast(F32),
                                      ALU.subtract).then_inc(q_lo, 1)
                quarters[0] = n

            rest_to(F_PARTS)

            def residual(first, order, b0=0):
                for j, (tb, half) in enumerate(order):
                    dve.wait_ge(res_ps, first + j + 1)
                    dst = h[:, tb, 512 * half:512 * half + 512]
                    dve.tensor_tensor(dst, dst, bank[:, b0 + j, :], ALU.add).then_inc(h_ready, 1)

            residual(0, [(tb, c) for c in range(2) for tb in range(TB)])
            norm(1)
            for k in range(KD):
                dve.wait_ge(f_x_ok, k // 2 * 2 + 2)
                last = dve.scalar_tensor_tensor(f_xlo[:, k, :], bank[:, k // 2, 256 * (k % 2):256 * (k % 2) + 256],
                                                gain[:, G_FFN0 + k:G_FFN0 + k + 1], f_xhi[:, k, :].bitcast(F32),
                                                ALU.mult, ALU.subtract)
            last.then_inc(xT_dve, 1)
            for n in range(N_GU + 1):
                rest_to(min(4 * n + 6, 4 * N_GU + F_PARTS))
                if n < N_GU:
                    for tb in range(TB):
                        j = 2 * n + tb
                        dve.wait_ge(sl_ready, j + 1)
                        if n >= 2:
                            dve.wait_ge(hT_ps, n - 1)
                        dve.tensor_tensor(f_hm[:, n % 2, tb, :], f_sl[:, j % 4, :], bank[:, j % 4, 256:512],
                                          ALU.mult).then_inc(hm_ready, 1)
                if n:
                    dve.wait_ge(f_h_ok, n)
                    dve.tensor_tensor(f_hlo[:, 2 * n - 2:2 * n, :].rearrange("p b t -> p (b t)"), bank[:, 4 + (n - 1) % 2, :],
                                      f_hhi[:, 2 * n - 2:2 * n, :].rearrange("p b t -> p (b t)").bitcast(F32),
                                      ALU.subtract).then_inc(hT_ready, 1)
            rest_to(N_QUART)
            residual(4, [(0, 0), (0, 1), (1, 0), (1, 1)])
            norm(2)
            transposed(2, G_MIX1)
            dve.wait_ge(xT_act, 2)
            transposed(2, G_KV, b_xk, (0, 1, 2, 3), xT_dve)

            def normed(j, n, width, job_sem, ss, rs, st, src, dst, told, pos):
                dve.wait_ge(job_sem, j + 1)
                dve.tensor_reduce(small[:, st:st + n], b_sq[:, 0:n * width].rearrange("p (n d) -> p n d", n=n),
                                  AX.X, ALU.add).then_inc(ss, 1)
                dve.wait_ge(rs, j + 1)
                dve.tensor_tensor(dst[:, :, 0:DH], src.rearrange("p (n d) -> p n d", n=n),
                                  small[:, st + 2 * n:st + 3 * n].unsqueeze(2).broadcast_to([P, n, DH]), ALU.mult)
                dve.tensor_copy(dst[:, :, DH:DA], pos).then_inc(told, 1)

            dve.memset(b_hid, 0.0).then_inc(init_ok, 1)
            for j in range(4):
                br, tb = divmod(j, 2)
                if j >= 2:
                    dve.wait_ge(kT_ps, j - 1)
                pos = cf[:, C_KPOS + 2 * tb:C_KPOS + 2 * tb + 2].unsqueeze(1).broadcast_to([P, NG, 2])
                normed(j, NG, DH, kv_sq, kv_ss, kv_rs, S_K + 12 * j, bank[:, (j + 2) % 4, 0:256],
                       b_aug[:, j % 2, 0:NG, :], kv_norm_ok, pos)
            for j in range(4):
                br, tb = divmod(j, 2)
                dve.wait_ge(kT_ps, j + 1)
                dve.tensor_scalar(b_kT[0:DA, br, :, P * tb:P * tb + P],
                                  bank[0:DA, 4 + j, :].rearrange("p (g t) -> p g t", g=NG),
                                  gnar[0:DA, GK + 1 + br:GK + 2 + br], None, ALU.mult).then_inc(kT_ready, 1)
            for tb in range(TB):
                dve.wait_ge(cT_ps, tb + 1)
                dve.tensor_copy(b_cT[:, :, P * tb:P * tb + P],
                                bank[:, tb, :].rearrange("p (g t) -> p g t", g=NG)).then_inc(cT_ready, 1)
            dve.wait_ge(pos_ps, 1)
            dve.tensor_copy(b_posT, bank[:, 2, 0:CB]).then_inc(pos_ready, 1)
            dve.wait_ge(cT_ready, 2)
            dve.wait_ge(pos_ready, 1)
            for g in range(NG):
                for par in range(2):
                    k = (NCMP + 1 - par) // 2
                    src = b_cT[:, g, CS * par:CS * par + 32 * k].rearrange("p (i j) -> p j i", j=32)
                    dst = b_cin[:, :, g, par:NCMP:2]
                    last = dve.tensor_tensor(dst, src, b_posT.unsqueeze(2).broadcast_to([P, CB, k]), ALU.add)
            last.then_inc(cin_ready, 1)
            dve.wait_ge(init_ok, 1)
            dve.wait_ge(hsT_ps, 2)
            for kv in range(2):
                last = dve.tensor_copy(
                    b_hid[:, kv, :, :].rearrange("p n (g c) -> p n g c", g=NG)[:, :, :, 0:NCMP],
                    bank[:, 7, 256 * kv:256 * kv + 256].rearrange("p (n x) -> p n x", n=2)[:, :, 0:NG * NCMP]
                    .rearrange("p n (g c) -> p n g c", g=NG))
            last.then_inc(hid_ready, 1)
            dve.wait_ge(kc_rs, 1)
            dve.wait_ge(kvc_ps, 2)
            dve.tensor_copy(b_vc, bank[:, 6, DH:2 * DH]).then_inc(kvc_ready, 1)
            dve.tensor_scalar(b_kca[:, 0:DH], bank[:, 6, 0:DH], small[:, S_C + 2:S_C + 3], None, ALU.mult)
            dve.tensor_copy(b_kca[:, DH:DA], cf[:, C_CPOS:C_CPOS + 2]).then_inc(kca_ready, 1)
            dve.wait_ge(kcT_ps, 1)
            dve.tensor_scalar(b_kc[0:DA, :], bank[0:DA, 5, 0:P], gnar[0:DA, GK:GK + 1], None,
                              ALU.mult).then_inc(kcT_ready, 1)
            for tb in range(TB):
                dve.wait_ge(gate_exp, tb + 1)
                step(dve.tensor_scalar(b_gate[:, tb, :], b_gate[:, tb, :], 1.0, None, ALU.add))
                step(dve.reciprocal(b_gate[:, tb, :], b_gate[:, tb, :]))
            for j in range(5):
                if j < 4:
                    it, tb = divmod(j, 2)
                    if j >= 2:
                        dve.wait_ge(qT_ps, 2 * (j - 1))
                    else:
                        dve.wait_ge(kT_ps, 4)
                    pos = cf[:, C_QPOS + 2 * (NH * tb + 8 * it):C_QPOS + 2 * (NH * tb + 8 * it) + 16]
                    normed(j, 8, DH, q_sq, q_ss, q_rs, S_Q + 24 * j, bank[:, j, :], b_aug[:, j % 2, :, :],
                           qa_ready, pos.rearrange("p (n w) -> p n w", w=2))
                if j:
                    it, tb = divmod(j - 1, 2)
                    for a in range(2):
                        dve.wait_ge(qT_ps, 2 * (j - 1) + a + 1)
                        hh = 8 * it + 4 * a
                        dve.tensor_scalar(b_qT[0:DA, hh:hh + 4, P * tb:P * tb + P],
                                          bank[0:DA, 4 + (2 * (j - 1) + a) % 4, :].rearrange("p (n t) -> p n t", n=4),
                                          gnar[0:DA, GQ:GQ + 1], None, ALU.mult).then_inc(qT_ready, 1)
            for tb in range(TB):
                st = S_CM + 48 * tb
                cp = b_cp
                dve.wait_ge(cs_ps, tb + 1)
                if tb:
                    dve.wait_ge(cpT_ps, tb)
                step(dve.tensor_tensor(cp, bank[:, tb, :].rearrange("p (n c) -> p n c", n=NH),
                                       cf[:, C_CMASK + 32 * tb:C_CMASK + 32 * tb + 32].unsqueeze(1)
                                       .broadcast_to([P, NH, 32]), ALU.add))
                step(dve.tensor_reduce(small[:, st:st + 16], cp, AX.X, ALU.max))
                step(dve.tensor_scalar(small[:, st:st + 16], small[:, st:st + 16], NEG / 10, None, ALU.max))
                dve.tensor_tensor(cp, cp, small[:, st:st + 16].unsqueeze(2).broadcast_to([P, NH, 32]),
                                  ALU.subtract).then_inc(cs_shift, 1)
                dve.wait_ge(cs_exp, tb + 1)
                step(dve.tensor_reduce(small[:, st + 16:st + 32], cp, AX.X, ALU.add))
                step(dve.tensor_scalar(small[:, st + 16:st + 32], small[:, st + 16:st + 32], TINY, None, ALU.max))
                step(dve.reciprocal(small[:, st + 16:st + 32], small[:, st + 16:st + 32]))
                gt = b_gate[:, tb, :].rearrange("p (g j b) -> p j g b", g=NG, b=3)[:, :, :, 0]
                sj = small[:, st + 16:st + 32].rearrange("p (j g) -> p j g", j=GRP)
                step(dve.tensor_tensor(sj, sj, gt, ALU.mult))
                dve.tensor_tensor(cp, cp, small[:, st + 16:st + 32].unsqueeze(2).broadcast_to([P, NH, 32]),
                                  ALU.mult).then_inc(cp_ready, 1)
                dve.wait_ge(cpT_ps, tb + 1)
                dve.tensor_copy(b_cpT[:, tb, 0:4, :], bank[:, 2 + tb, :].rearrange("p (j t) -> p j t", j=4)
                                ).then_inc(cpT_ready, 1)
            for g in range(NG):
                dve.wait_ge(co_ps, 8)
                dve.tensor_copy(b_o[:, :, 256 * g:256 * g + 256],
                                bank[:, 4 + g, :].rearrange("p (b d) -> p b d", b=TB)).then_inc(co_taken, 1)
            dve.wait_ge(co_taken, 4)

            def add_out(u):
                br, g, tb = u // 8, u // 2 % 4, u % 2
                st = S_A + 16 * (u % 2)
                dve.wait_ge(av_ps, u + 1)
                o3 = b_o[:, tb, 256 * g:256 * g + 256].rearrange("p (j d) -> p j d", j=GRP)
                t3 = b_t.rearrange("p (j d) -> p j d", j=GRP)
                dve.tensor_tensor(t3, bank[:, 6 + u % 2, 0:256].rearrange("p (j d) -> p j d", j=GRP),
                                  small[:, st + 8:st + 12].unsqueeze(2).broadcast_to([P, GRP, DH]),
                                  ALU.mult).then_inc(av_taken, 1)
                dve.wait_ge(av_taken, u + 1)
                dve.tensor_tensor(o3, o3, t3, ALU.add).then_inc(o_added, 1)
                dve.wait_ge(o_added, u + 1)

            def probs(u):
                br, g, tb = u // 8, u // 2 % 4, u % 2
                st = S_A + 16 * (u % 2)
                dve.wait_ge(p_ready, u + 1)
                step(dve.reciprocal(small[:, st + 8:st + 12], small[:, st + 4:st + 8]))
                gt = b_gate[:, tb, :].rearrange("p (h b) -> p h b", b=3)[:, GRP * g:GRP * g + GRP, 1 + br]
                step(dve.tensor_tensor(small[:, st + 8:st + 12], small[:, st + 8:st + 12], gt, ALU.mult))
                dve.wait_ge(pT_ps, u + 1)
                if u >= 2:
                    dve.wait_ge(av_ps, u - 1)
                if tb == 0:
                    src, dst = bank[:, 3, :], b_pT[:, 0, 0:4, :]
                    src = src.rearrange("p (j t) -> p j t", j=4)
                else:
                    src, dst = bank[:, 4:6, :].rearrange("p b (j t) -> p (b j) t", j=4), b_pT[:, 1, :, :]
                dve.tensor_copy(dst, src).then_inc(pT_ready, 1)

            def maxima(u):
                st = S_A + 16 * (u % 2)
                src = (bank[:, 0, :].rearrange("p (j k) -> p j k", j=4) if u % 2 == 0
                       else bank[:, 1:3, :].rearrange("p b (j k) -> p (b j) k", j=2))
                dve.wait_ge(s_ps, u + 1)
                step(dve.tensor_reduce(small[:, st:st + 4], src, AX.X, ALU.max))
                dve.tensor_scalar(small[:, st:st + 4], small[:, st:st + 4], -1.0, None, ALU.mult).then_inc(max_ready, 1)

            maxima(0)
            for u in range(17):
                if u < 15:
                    maxima(u + 1)
                if u:
                    add_out(u - 1)
                if u < 16:
                    probs(u)
            for b in (0, 2):
                dve.wait_ge(bo_ps, b + 1)
                for k in (2 * b, 2 * b + 1):
                    last = dve.tensor_copy(xT[:, k, :], bank[:, b, 256 * (k % 2):256 * (k % 2) + 256])
            last.then_inc(bo_dve, 1)
            residual(8, [(tb, c) for c in range(2) for tb in range(TB)], 4)
            norm(3)
            transposed(3, G_FFN1)
            step(dve.memset(arena[:, 0:8 * (NE + 1)], 0.0))
            for tb in range(TB):
                lg, sel, wt = m_lg[:, tb, :], m_sel[:, tb, 0:NE], m_wt[:, tb, 0:NE]
                dve.wait_ge(lg_ps, 2)
                step(dve.tensor_copy(lg, bank[:, 4, 8 * tb:8 * tb + 8]))
                mine, other = lg.unsqueeze(2).broadcast_to([P, NE, NE]), lg.unsqueeze(1).broadcast_to([P, NE, NE])
                step(dve.tensor_tensor(m_cmp, other, mine, ALU.is_equal))
                step(dve.tensor_tensor(m_cmp, m_cmp, cf[:, C_TIE:C_TIE + 64].rearrange("p (e j) -> p e j", e=NE), ALU.mult))
                step(dve.tensor_tensor(m_cmp2, other, mine, ALU.is_gt))
                step(dve.tensor_tensor(m_cmp, m_cmp, m_cmp2, ALU.add))
                step(dve.tensor_reduce(sel, m_cmp, AX.X, ALU.add))
                step(dve.tensor_scalar(sel, sel, 2.0, None, ALU.is_lt))
                step(dve.tensor_reduce(small[:, S_L + tb:S_L + tb + 1], lg, AX.X, ALU.max))
                dve.tensor_scalar(lg, lg, small[:, S_L + tb:S_L + tb + 1], None, ALU.subtract).then_inc(lg_shift, 1)
                dve.wait_ge(lg_exp, tb + 1)
                step(dve.tensor_tensor(wt, lg, sel, ALU.mult))
                step(dve.tensor_reduce(small[:, S_L + 2 + tb:S_L + 3 + tb], wt, AX.X, ALU.add))
                step(dve.reciprocal(small[:, S_L + 2 + tb:S_L + 3 + tb], small[:, S_L + 2 + tb:S_L + 3 + tb]))
                dve.tensor_scalar(wt, wt, small[:, S_L + 2 + tb:S_L + 3 + tb], None, ALU.mult).then_inc(sel_ready, 1)
            dve.wait_ge(rank_ps, 1)
            for q in range(2):
                ins = dve.tensor_scalar(m_pos[:, 2 * q:2 * q + 2, 0:NE], bank[:, 5, 0:16].rearrange("p (b e) -> p b e", b=TB),
                                        -float(P * q), None, ALU.add)
            ins.then_inc(route_ready, 1)
            dve.tensor_reduce(small[:, S_L + 4:S_L + 5], bank[:, 5, 16:24], AX.X, ALU.max).then_inc(route_ready, 1)
            dve.wait_ge(route_ready, 2)
            dve.tensor_copy(flag[:, :], small[:, S_L + 4:S_L + 5]).then_inc(route_ready, 1)

            dve.memset(m_PT, 0.0)
            dve.memset(small[:, 504:505], 0.0).then_inc(w_free, PARTS)
            splits = [0]

            def split_to(n, E):
                for s0 in range(splits[0], n):
                    s, E1 = split_part(dve, s0, E)
                    dve.wait_ge(hi_ready, E1 * HALVES + (s + 1))
                    dve.tensor_tensor(w_lo[s % PARTS][:, :], raw[:, s % RAWS, :], w_hi[s % PARTS][:, :].bitcast(F32),
                                      ALU.subtract).then_inc(lo_ready, 1)
                splits[0] = n

            def select(e, G, q):
                iota = cf[:, C_IOTA:C_IOTA + P]
                for tb in range(TB):
                    dve.tensor_scalar(m_P[:, tb, :], iota, m_pos[:, 2 * q + tb, bass.ds(e, 1)],
                                      m_sel[:, tb, bass.ds(e, 1)], ALU.is_equal, ALU.mult).then_inc(P_made, 1)
                dve.wait_ge(P_made, G * 2 + 2)
                for tb in range(TB):
                    last = dve.tensor_scalar(m_PW[:, tb, :], m_P[:, tb, :], m_wt[:, tb, bass.ds(e, 1)],
                                             None, ALU.mult)
                last.then_inc(P_ready, 1)

            def gathered(half, G):
                dve.wait_ge(x_hi_ok, G * 2 + (half + 1))
                for k in range(4 * half, 4 * half + 4):
                    last = dve.scalar_tensor_tensor(x_lo[:, k, :], bank[:, 7, P * (k % 4):P * (k % 4) + P],
                                                    gain[:, G_FFN1 + k:G_FFN1 + k + 1], x_hi[:, k, :].bitcast(F32),
                                                    ALU.mult, ALU.subtract)
                last.then_inc(x_lo_ok, 1)

            def hidden(c, E):
                dve.wait_ge(t_hi_ok, E * NCH + (c + 1))
                dve.tensor_tensor(t_lo[:, c % 2, :, :].rearrange("p b t -> p (b t)"), bank[:, 4, :],
                                  t_hi[:, c % 2, :, :].bitcast(F32).rearrange("p b t -> p (b t)"),
                                  ALU.subtract).then_inc(t_lo_ok, 1)

            def scattered(Z):
                for j, b in enumerate(SCATTER_BANKS):
                    tb, half = divmod(j, 2)
                    dve.wait_ge(sc_ps, Z * 4 + (j + 1))
                    dst = h[:, tb, 512 * half:512 * half + 512]
                    dve.tensor_tensor(dst, dst, bank[:, b, :], ALU.add).then_inc(sc_taken, 1)

            def expert(e, E, q):
                for c in range(NCH):
                    if c:
                        split_to(2 * gu_item(c, 0) + 1 + PARTS, E)
                        hidden(c - 1, E)
                    s = 2 * gu_item(c, 1) + 1
                    split_to(s + PARTS, E)
                    dve.wait_ge(e_sl, E * NCH + (c + 1))
                    dve.wait_ge(*used(s, E))
                    dve.tensor_tensor(m_h[:, c % 2, :], m_sl[:, c % 2, :], bank[:, 2 * (c % 2) + 1, :],
                                      ALU.mult).then_inc(e_h, 1)
                    if c == 0:
                        scattered(E + q)
                    if c == 2:
                        dve.wait_ge(PT_ps, E + 1)
                        select(e + 1, E + (1 + q), q)
                gathered(0, E + (1 + q))
                split_to(2 * down_item(NCH - 2) + 1 + PARTS, E)
                hidden(NCH - 1, E)
                gathered(1, E + (1 + q))
                split_to(HALVES - 1 + PARTS, E)
                splits[0] = PARTS - 1

            def all_experts(E0, q):
                dve.memset(m_y, 0.0).then_inc(y_ready, 1)
                select(0, E0 + q, q)
                gathered(0, E0 + q)
                gathered(1, E0 + q)
                with dve.Fori(0, NE) as e:
                    expert(e, e + E0, q)
                scattered(E0 + NE + q)

            split_to(PARTS - 1, 0)
            all_experts(0, 0)
            dve.wait_ge(route_ready, 3)
            most = dve.value_load(flag[0:1, 0:1], min_val=0, max_val=T)
            with dve.If(most > P):
                all_experts(NE, 1)
            dve.memset(small[:, 500:501], 0.0).then_inc(h_ready, 1)

        @block.tensor
        def _(pe):
            mm, tp = nc.tensor.matmul, nc.tensor.transpose
            pe.wait_ge(const_in, 32)

            def transposed(src, told, b0=0):
                for tb in range(TB):
                    for k in range(KD):
                        last = tp(bank[:, b0 + k // 2, 256 * (k % 2) + P * tb:256 * (k % 2) + P * tb + P],
                                  src[:, tb, P * k:P * k + P], ident)
                        if tb and k % 2:
                            last.then_inc(told, 1)

            def norm(i):
                for tb in range(TB):
                    pe.wait_ge(xs_ready, 2 * i + tb + 1)
                    for k in range(KD):
                        last = tp(bank[:, k // 2, 256 * (k % 2) + P * tb:256 * (k % 2) + P * tb + P],
                                  xs[:, tb, P * k:P * k + P], ident)
                        if tb and k % 2:
                            last.then_inc(xT_ps, 1)

            def arrived(i):
                pe.wait_ge(slot_full[i % SLOTS], full(i))

            def cols(i):
                return slot(i).rearrange("p (k c) -> p k c", k=KD)

            norm(0)
            pe.wait_ge(gain_in, 96)
            pe.wait_ge(gains_ps, 1)
            tp(bank[:, 4, 0:R_GAIN], arena[0:R_GAIN, 0:P], ident[0:R_GAIN, 0:R_GAIN])
            tp(bank[0:DA, 4, 64:68], arena[0:4, 128:128 + DA], ident[0:4, 0:4]).then_inc(gains_ps, 1)
            pe.wait_ge(xT_dve, 1)
            pe.wait_ge(xT_act, 1)
            for j in range(8):
                i = j // 2
                if j % 2 == 0:
                    arrived(i)
                if j >= 4:
                    pe.wait_ge(f_taken, j - 3)
                for hh in range(2):
                    c0 = (2 * (j % 2) + hh) * P
                    for k in range(KD):
                        last = mm(bank[:, j % 4, 256 * hh:256 * hh + 256], cols(i)[:, k, c0:c0 + P],
                                  xT[:, k, :], start=k == 0, stop=k == KD - 1)
                last.then_inc(proj_ready, 1)

            def pairs(n, grp):
                m = LEVELS[n]
                if n == 0:
                    pe.wait_ge(key_ok, 4)
                    pe.wait_ge(qv_taken, 4)
                else:
                    pe.wait_ge(ops_ready, 2 * (n - 1) + grp + 1)
                    pe.wait_ge(pair_taken, 2 * (n - 1) + grp + 1)
                for tb in range(TB):
                    for hh in range(4):
                        hd = 4 * grp + hh
                        b = 4 + 2 * grp + tb
                        if n == MLEV:
                            if tb == 0:
                                last = mm(bank[:, b, P * hh:P * hh + P], a_kl[:, hd, 0:P], a_ql[:, hd, P:T],
                                          start=True, stop=True)
                            continue
                        ts = slice(P * tb, P * tb + P)
                        last = mm(bank[:, b, P * hh:P * hh + P], (a_kl if m > 1 else a_k)[:, hd, ts],
                                  (a_ql if m else a_q)[:, hd, ts], start=True, stop=True)
                last.then_inc(pair_ps, 1)

            for n in range(9):
                if n < 8:
                    it, tb = divmod(n, 2)
                    if tb == 0:
                        arrived(4 + it)
                    pe.wait_ge(qv_taken, n + 1)
                    for k in range(KD):
                        last = mm(bank[:, n % 4, :], xT[:, k, P * tb:P * tb + P], cols(4 + it)[:, k, :],
                                  start=k == 0, stop=k == KD - 1)
                    last.then_inc(proj_ready, 1)
                for grp in range(2):
                    pairs(n, grp)
            pe.wait_ge(qv_taken, 12)
            for j in range(4):
                tb, grp = divmod(j, 2)
                pe.wait_ge(pair_taken, 17 + grp)
                for hh in range(4):
                    cs = slice(512 * grp + P * hh, 512 * grp + P * hh + P)
                    dst = bank[:, j, P * hh:P * hh + P]
                    if tb:
                        mm(dst, a_so[:, grp, hh, :], a_v[:, 0, cs], start=True, stop=False)
                    last = mm(dst, a_st[:, grp, tb, hh, :], a_v[:, tb, cs], start=not tb, stop=True)
                last.then_inc(o_ps, 1)
            pe.wait_ge(on_ready, 4)
            transposed(a_on, oT_ps, 4)
            pe.wait_ge(oT_dve, 1)
            pe.wait_ge(oT_act, 1)

            def out_product(i0, lhs, b0=0):
                for c in range(2):
                    arrived(i0 + c)
                    for tb in range(TB):
                        for k in range(KD):
                            last = mm(bank[:, b0 + 2 * c + tb, :], lhs[:, k, P * tb:P * tb + P], cols(i0 + c)[:, k, :],
                                      start=k == 0, stop=k == KD - 1)
                        last.then_inc(res_ps, 1)

            out_product(I_HOUT, a_oT)
            pe.wait_ge(h_ready, 4)
            norm(1)
            pe.wait_ge(xT_dve, 2)
            def parts(d, width):
                pe.wait_ge(q_lo, d + 1)
                return [v.rearrange("p (k c) -> p k c", c=width) for v in (f_whi[d % F_PARTS][:, :], quarter(d)[1])]

            def split_product(dst, hi, lo, w, k, start, stop):
                for n, (x_, w_) in enumerate(((hi, w[0]), (hi, w[1]), (lo, w[0]))):
                    done = [mm(out_, x_, w_[:, k, 512 * b:512 * b + 512], start=start and n == 0, stop=stop and n == 2)
                            for b, out_ in enumerate(dst)]
                return done

            for n in range(N_GU + 1):
                if n < N_GU:
                    if n >= 2:
                        pe.wait_ge(hm_ready, 2 * n - 2)
                    for a in range(4):
                        w = parts(4 * n + a, 512)
                        for k in (2 * a, 2 * a + 1):
                            for tb in range(TB):
                                last = split_product([bank[:, (2 * n + tb) % 4, :]], f_xhi[:, k, P * tb:P * tb + P],
                                                     f_xlo[:, k, P * tb:P * tb + P], w, k % 2, k == 0, k == KD - 1)
                                if k == KD - 1:
                                    last[0].then_inc(gu_ps, 1)
                        if a < 3:
                            last[0].then_inc(q_used, 1)
                if n:
                    pe.wait_ge(hm_ready, 2 * n)
                    if n > 2:
                        pe.wait_ge(hT_ready, n - 2)
                    for b in range(2):
                        for tb in range(TB):
                            last = tp(bank[:, 4 + (n - 1) % 2, 256 * b + P * tb:256 * b + P * tb + P],
                                      f_hm[:, (n - 1) % 2, tb, P * b:P * b + P], ident)
                    last.then_inc(hT_ps, 1)
            pe.wait_ge(hT_ready, N_GU)
            for f in range(2 * N_GU):
                w = parts(4 * N_GU + f, D)
                for tb in range(TB):
                    last = split_product([bank[:, 2 * tb + c, :] for c in range(2)], f_hhi[:, f, P * tb:P * tb + P],
                                         f_hlo[:, f, P * tb:P * tb + P], w, 0, f == 0, f == 2 * N_GU - 1)
                    if f == 2 * N_GU - 1:
                        for made in last:
                            made.then_inc(res_ps, 1)
                if f < 2 * N_GU - 1:
                    last[1].then_inc(q_used, 1)
            pe.wait_ge(h_ready, 8)
            norm(2)
            pe.wait_ge(xT_dve, 4)
            pe.wait_ge(xT_act, 2)
            for j in range(6):
                it, tb = divmod(j, 2)
                if tb == 0:
                    arrived(I_KV + it)
                if j >= 4:
                    pe.wait_ge(kv_raw, j - 3)
                for k in range(KD):
                    last = mm(bank[:, j % 4, :], b_xk[:, k, P * tb:P * tb + P], cols(I_KV + it)[:, k, :],
                              start=k == 0, stop=k == KD - 1)
                last.then_inc(kv_ps, 1)
            for j in range(4):
                pe.wait_ge(kv_norm_ok, j + 1)
                for g in range(NG):
                    last = tp(bank[0:DA, 4 + j, P * g:P * g + P], b_aug[:, j % 2, g, :], ident)
                last.then_inc(kT_ps, 1)
            pe.wait_ge(misc_in, 80)
            pe.wait_ge(kv_raw, 2)
            for tb in range(TB):
                for g in range(NG):
                    last = tp(bank[:, tb, P * g:P * g + P], b_raw[:, tb, P * g:P * g + P], ident)
                last.then_inc(cT_ps, 1)
            tp(bank[:, 2, 0:CB], b_pos[0:CB, :], ident[0:CB, 0:CB]).then_inc(pos_ps, 1)
            pe.wait_ge(cin_ready, 1)
            pe.wait_ge(kT_ready, 2)
            arrived(I_CMP)
            arrived(I_CMP + 1)
            for kv in range(2):
                ps = slice(DH * kv, DH * kv + DH)
                for j in range(CB):
                    w = slot(I_CMP + j // 16).rearrange("p (j c) -> p j c", j=16)
                    last = mm(bank[0:NG * NCMP, 4 + kv, 0:CH], b_cin[ps, j, :, :].rearrange("p g c -> p (g c)"),
                              w[ps, j % 16, :], start=j == 0, stop=j == CB - 1)
                last.then_inc(hid_ps, 1)
            pe.wait_ge(kT_ready, 4)
            for kv in range(2):
                pe.wait_ge(hs_ready, kv + 1)
                for half in range(2):
                    n = 2 * kv + half
                    last = tp(bank[:, 7, P * n:P * n + NG * NCMP], b_hs[0:NG * NCMP, kv, P * half:P * half + P],
                              ident[0:NG * NCMP, 0:NG * NCMP])
                last.then_inc(hsT_ps, 1)
            pe.wait_ge(hid_ready, 1)
            for kv in range(2):
                for half in range(2):
                    last = mm(bank[:, 6, DH * kv:DH * kv + DH], b_hid[:, kv, half, :], b_w2[:, kv, half, :],
                              start=half == 0, stop=half == 1)
                last.then_inc(kvc_ps, 1)
            for tb in range(TB):
                for k in range(KD):
                    last = mm(bank[:, 7, 64 * tb:64 * tb + 48], xT[:, k, P * tb:P * tb + P], b_wg[:, k, :],
                              start=k == 0, stop=k == KD - 1)
                last.then_inc(gate_ps, 1)
            pe.wait_ge(pos_ready, 1)
            for j in range(4):
                it, tb = divmod(j, 2)
                if tb == 0:
                    arrived(I_Q + it)
                for k in range(KD):
                    last = mm(bank[:, j, :], xT[:, k, P * tb:P * tb + P], cols(I_Q + it)[:, k, :],
                              start=k == 0, stop=k == KD - 1)
                last.then_inc(q_ps, 1)
            pe.wait_ge(kca_ready, 1)
            tp(bank[0:DA, 5, 0:P], b_kca, ident).then_inc(kcT_ps, 1)
            pe.wait_ge(kcT_ready, 1)
            pe.wait_ge(gate_exp, 2)
            for j in range(4):
                pe.wait_ge(qa_ready, j + 1)
                for a in range(2):
                    n = 2 * j + a
                    if n >= 4:
                        pe.wait_ge(qT_ready, n - 3)
                    for hh in range(4):
                        last = tp(bank[0:DA, 4 + n % 4, P * hh:P * hh + P], b_aug[:, j % 2, 4 * a + hh, :], ident)
                    last.then_inc(qT_ps, 1)
            pe.wait_ge(qT_ready, 8)
            for tb in range(TB):
                for j in range(GRP):
                    for g in range(NG):
                        last = mm(bank[:, tb, 32 * (NG * j + g):32 * (NG * j + g) + 32],
                                  b_qT[0:DA, GRP * g + j, P * tb:P * tb + P], b_kc[0:DA, 32 * g:32 * g + 32],
                                  start=True, stop=True)
                last.then_inc(cs_ps, 1)
            for tb in range(TB):
                pe.wait_ge(cp_ready, tb + 1)
                for j in range(GRP):
                    last = tp(bank[:, 2 + tb, P * j:P * j + P],
                              b_cp[:, NG * j:NG * j + NG, :].rearrange("p g c -> p (g c)"), ident)
                last.then_inc(cpT_ps, 1)
            for tb in range(TB):
                pe.wait_ge(cpT_ready, tb + 1)
                for g in range(NG):
                    ps = slice(32 * g, 32 * g + NCMP)
                    for j in range(GRP):
                        at = 256 * tb + DH * j
                        last = mm(bank[:, 4 + g, at:at + DH], b_cpT[ps, tb, j, :], b_vc[ps, :],
                                  start=True, stop=True)
                    last.then_inc(co_ps, 1)
            pe.wait_ge(co_taken, 4)

            def scores(u):
                br, g, tb = u // 8, u // 2 % 4, u % 2
                if u >= 2:
                    pe.wait_ge(p_ready, u - 1)
                for j in range(GRP):
                    if tb == 0:
                        dst = bank[:, 0, P * j:P * j + P]
                    else:
                        dst = bank[:, 1 + j // 2, T * (j % 2):T * (j % 2) + T]
                    n = P * (tb + 1)
                    mm(dst, b_qT[0:DA, GRP * g + j, P * tb:P * tb + P], b_kT[0:DA, br, g, 0:n],
                       start=True, stop=False)
                    last = mm(dst, cb[:, 0:P], cb[:, 3 * P - n:3 * P], start=False, stop=True)
                last.then_inc(s_ps, 1)

            def turn(u):
                tb = u % 2
                pe.wait_ge(p_ready, u + 1)
                if u >= 2:
                    pe.wait_ge(pT_ready, u - 1)
                for j in range(GRP):
                    for kb in range(tb + 1):
                        n = (tb + 1) * j + kb
                        b = 3 if tb == 0 else 4 + n // 4
                        last = tp(bank[:, b, P * (n % 4):P * (n % 4) + P], b_p[:, tb, j, P * kb:P * kb + P], ident)
                last.then_inc(pT_ps, 1)

            def attend(u):
                br, g, tb = u // 8, u // 2 % 4, u % 2
                pe.wait_ge(pT_ready, u + 1)
                if u >= 2:
                    pe.wait_ge(av_taken, u - 1)
                for j in range(GRP):
                    dst = bank[:, 6 + u % 2, DH * j:DH * j + DH]
                    for kb in range(tb + 1):
                        last = mm(dst, b_pT[:, tb, (tb + 1) * j + kb, :], b_v[:, br, kb, DH * g:DH * g + DH],
                                  start=kb == 0, stop=kb == tb)
                last.then_inc(av_ps, 1)

            scores(0)
            for u in range(17):
                if u < 15:
                    scores(u + 1)
                if u:
                    attend(u - 1)
                if u < 16:
                    turn(u)
            pe.wait_ge(o_added, 16)
            transposed(b_o, bo_ps)
            pe.wait_ge(bo_dve, 1)
            pe.wait_ge(bo_act, 1)
            out_product(I_OUT, xT, 4)
            pe.wait_ge(h_ready, 12)
            norm(3)
            pe.wait_ge(xT_dve, 5)
            pe.wait_ge(xT_act, 3)
            pe.wait_ge(wr_in, 16)
            for tb in range(TB):
                for k in range(KD):
                    last = mm(bank[:, 4, 8 * tb:8 * tb + 8], xT[:, k, P * tb:P * tb + P], m_wr[:, k, :],
                              start=k == 0, stop=k == KD - 1)
                last.then_inc(lg_ps, 1)
            pe.wait_ge(sel_ready, 2)
            tri, ones = cf[:, C_TRI:C_TRI + P], cf[:, C_ONE:C_ONE + 1].broadcast_to([P, P])
            mm(bank[:, 5, 0:8], tri, m_sel[:, 0, 0:NE], start=True, stop=True)
            mm(bank[:, 5, 8:16], ones, m_sel[:, 0, 0:NE], start=True, stop=False)
            mm(bank[:, 5, 8:16], tri, m_sel[:, 1, 0:NE], start=False, stop=True)
            mm(bank[:, 5, 16:24], ones, m_sel[:, 0, 0:NE], start=True, stop=False)
            mm(bank[:, 5, 16:24], ones, m_sel[:, 1, 0:NE], start=False, stop=True).then_inc(rank_ps, 1)
            pe.wait_ge(route_ready, 2)

            def gather(half, G):
                for k in range(4 * half, 4 * half + 4):
                    for tb in range(TB):
                        last = mm(bank[:, 7, P * (k % 4):P * (k % 4) + P], xs[:, tb, P * k:P * k + P],
                                  m_P[:, tb, :], start=tb == 0, stop=tb == 1)
                last.then_inc(x_ps, 1)

            def scatter(Z):
                for j, b in enumerate(SCATTER_BANKS):
                    tb, half = divmod(j, 2)
                    mm(bank[:, b, :], m_PT[:, P * tb:P * tb + P], m_y[:, 512 * half:512 * half + 512],
                       start=True, stop=True).then_inc(sc_ps, 1)

            def product(dst, s, E, hi, lo, width, start, stop):
                pe.wait_ge(lo_ready, E * HALVES + (s + 1))
                wh, wl = part_of(s, w_hi), part_of(s, w_lo)
                for k in range(HALF // width):
                    for n, (x_, w) in enumerate(((hi, wh), (hi, wl), (lo, wh))):
                        for b, out_ in enumerate(dst):
                            last = mm(out_, x_[k], w[:, k, 512 * b:512 * b + 512],
                                      start=start and k == 0 and n == 0,
                                      stop=stop and k == HALF // width - 1 and n == 2)
                last.then_inc(w_free, 1)

            def wide(c, up, E):
                for a in range(2):
                    ks = range(4 * a, 4 * a + 4)
                    product([bank[:, 2 * (c % 2) + up, :]], 2 * gu_item(c, up) + a, E,
                            [x_hi[:, k, :] for k in ks], [x_lo[:, k, :] for k in ks], 512, a == 0, a == 1)

            def turn(c, E):
                pe.wait_ge(e_h, E * NCH + (c + 1))
                for b in range(4):
                    last = tp(bank[:, 4, P * b:P * b + P], m_h[:, c % 2, P * b:P * b + P], ident)
                last.then_inc(e_hT_ps, 1)

            def down(c, E):
                pe.wait_ge(t_lo_ok, E * NCH + (c + 1))
                for a in range(2):
                    bs = range(2 * a, 2 * a + 2)
                    product([bank[:, 5, :], bank[:, 6, :]], 2 * down_item(c) + a, E,
                            [t_hi[:, c % 2, b, :] for b in bs], [t_lo[:, c % 2, b, :] for b in bs], D,
                            c == 0 and a == 0, c == NCH - 1 and a == 1)

            def expert(e, E, q):
                pe.wait_ge(x_lo_ok, E * 2 + (2 * q + 2))
                for c in range(NCH):
                    if c >= 2:
                        pe.wait_ge(e_h, E * NCH + (c - 1))
                    elif c == 1:
                        pe.wait_ge(sc_taken, E * 4 + (4 * q + 2))
                    wide(c, 0, E)
                    if c:
                        if c == 1:
                            pe.wait_ge(sc_taken, E * 4 + (4 * q + 3))
                        else:
                            pe.wait_ge(t_lo_ok, E * NCH + (c - 1))
                        turn(c - 1, E)
                    wide(c, 1, E)
                    if c == 0:
                        pe.wait_ge(y_ready, E + (1 + q))
                        scatter(E + q)
                    else:
                        if c == 1:
                            pe.wait_ge(sc_taken, E * 4 + (4 * q + 4))
                            for tb in range(TB):
                                last = tp(bank[:, 7, P * tb:P * tb + P], m_PW[:, tb, :], ident)
                            last.then_inc(PT_ps, 1)
                        if c == NCH - 1:
                            pe.wait_ge(P_ready, E + (2 + q))
                            pe.wait_ge(PT_ready, E + 1)
                            gather(0, E + (1 + q))
                        down(c - 1, E)
                pe.wait_ge(t_lo_ok, E * NCH + (NCH - 1))
                turn(NCH - 1, E)
                pe.wait_ge(x_lo_ok, E * 2 + (2 * q + 3))
                gather(1, E + (1 + q))
                down(NCH - 1, E)

            def all_experts(E0, q):
                pe.wait_ge(P_ready, E0 + q + 1)
                gather(0, E0 + q)
                pe.wait_ge(x_lo_ok, 2 * (E0 + q) + 1)
                gather(1, E0 + q)
                with pe.Fori(0, NE) as e:
                    expert(e, e + E0, q)
                pe.wait_ge(y_ready, E0 + NE + 1 + q)
                pe.wait_ge(x_lo_ok, 2 * (E0 + NE + q) + 2)
                scatter(E0 + NE + q)

            all_experts(0, 0)
            pe.wait_ge(route_ready, 3)
            most = pe.value_load(flag[0:1, 0:1], min_val=0, max_val=T)
            with pe.If(most > P):
                all_experts(NE, 1)


_INS = ["x", "norm_mix", "norm_ffn", "hgrn_w_in", "hgrn_w_out", "hgrn_g_norm", "kv_norm", "kv_w",
        "cmp_pos_k", "cmp_w1_k", "cmp_w2_k", "cmp_pos_v", "cmp_w1_v", "cmp_w2_v", "k_norm",
        "nsa_w_in", "nsa_w_out", "nsa_q_norm", "ffn_w_gu", "ffn_w_down", "moe_router", "moe_w_gu",
        "moe_w_down"]


def kernel(**inputs):
    import concourse.bacc as bacc
    from concourse.bass_utils import run_bass_kernel_spmd

    nc = bacc.Bacc("TRN2", target_bir_lowering=False, num_devices=1)
    arrays, args = {}, []
    for name in _INS:
        arrays[f"in_{name}"] = np.ascontiguousarray(inputs[name])
    for name, a in zip(("const_f32", "const_masks"), constants()):
        arrays[f"in_{name}"] = a
    for name, a in arrays.items():
        args.append(nc.dram_tensor(name, a.shape, mybir.dt.from_np(a.dtype), kind="ExternalInput").ap())
    args.append(nc.dram_tensor("out_h", (1, T, D), F32, kind="ExternalOutput").ap())
    trunk(nc, *args)
    result = run_bass_kernel_spmd(nc, [arrays], core_ids=[0])
    return result.results[0]["out_h"]
```
